# Optimizing a Trainium2 kernel written in Bass

```python
import jax, jax.numpy as jnp
from jax import lax
import numpy as np

D_MODEL = 1024
BATCH = 1
SEQ = 256
DEPTH = 2

EPS = 1e-6
D_FF = 2816
MLA_HEADS = 8
MLA_Q_LORA = 256
MLA_KV_LORA = 128
MLA_NOPE = 64
MLA_ROPE = 32
MLA_V = 64
MLA_QK = MLA_NOPE + MLA_ROPE
ROPE_BASE = 10000.0
ATTN_BLOCK = 128
GDN_HEADS = 8
GDN_DK = 64
GDN_DV = 64
GDN_CONV = 4
GDN_CHUNK = 64
GDN_QKV_W = GDN_HEADS * (2 * GDN_DK + GDN_DV)
SG_GROUPS = 8
SG_WIDTH = 2048
SG_CHUNK = 128
AB_WIDTHS = (MLA_Q_LORA, MLA_KV_LORA, MLA_ROPE, GDN_QKV_W, GDN_HEADS * GDN_DV, GDN_HEADS, GDN_HEADS)
IN_AB = sum(AB_WIDTHS)
MIX_AB = MLA_HEADS * MLA_V + GDN_HEADS * GDN_DV

kernel_name = "hybrid_mla_gdn_sgmlp_macaron"

def rms_norm(x, w):
    xf = x.astype(jnp.float32)
    y = xf * lax.rsqrt(jnp.mean(xf * xf, axis=-1, keepdims=True) + EPS)
    return (y * w.astype(jnp.float32)).astype(x.dtype)

def l2_norm(x):
    return x * lax.rsqrt(jnp.sum(x * x, axis=-1, keepdims=True) + EPS)

def swiglu(h, w_gate, w_up, w_down):
    return (jax.nn.silu(h @ w_gate) * (h @ w_up)) @ w_down

def rope_tables(positions):
    inv_freq = ROPE_BASE ** (-jnp.arange(0, MLA_ROPE, 2, dtype=jnp.float32) / MLA_ROPE)
    ang = positions.astype(jnp.float32)[..., None] * inv_freq
    return jnp.cos(ang)[:, :, None, :], jnp.sin(ang)[:, :, None, :]

def apply_rope(t, cos, sin):
    half = MLA_ROPE // 2
    t_nope, r1, r2 = t[..., :MLA_NOPE], t[..., MLA_NOPE:MLA_NOPE + half], t[..., MLA_NOPE + half:]
    c, s = cos.astype(t.dtype), sin.astype(t.dtype)
    return jnp.concatenate([t_nope, r1 * c - r2 * s, r2 * c + r1 * s], axis=-1)

def causal_block_attention(q, k, v):
    b, s, h, dq = q.shape
    dv = v.shape[-1]
    nb = s // ATTN_BLOCK
    scale = dq ** -0.5
    qb = q.astype(jnp.float32).reshape(b, nb, ATTN_BLOCK, h, dq).transpose(1, 0, 3, 2, 4)
    kh = k.astype(jnp.float32).transpose(0, 2, 1, 3)
    vh = v.astype(jnp.float32).transpose(0, 2, 1, 3)
    key_idx = jnp.arange(s)

    def one_block(args):
        q_blk, blk = args
        sc = jnp.einsum('bhqd,bhkd->bhqk', q_blk, kh) * scale
        q_idx = blk * ATTN_BLOCK + jnp.arange(ATTN_BLOCK)
        sc = jnp.where(key_idx[None, :] <= q_idx[:, None], sc, -jnp.inf)
        p = jax.nn.softmax(sc, axis=-1)
        return jnp.einsum('bhqk,bhkd->bhqd', p, vh)

    o = lax.map(one_block, (qb, jnp.arange(nb)))
    return o.transpose(1, 0, 3, 2, 4).reshape(b, s, h * dv).astype(v.dtype)

def causal_short_conv(x, w):
    kw, s = w.shape[0], x.shape[1]
    xp = jnp.pad(x, ((0, 0), (kw - 1, 0), (0, 0)))
    return sum(xp[:, j:j + s] * w[j] for j in range(kw))

def gated_delta_rule(q, k, v, beta, g):
    b, s, h, dk = q.shape
    dv = v.shape[-1]
    c = GDN_CHUNK
    n = s // c

    def chunks(t):
        return t.reshape(b, n, c, h, -1).transpose(0, 3, 1, 2, 4)

    q, k, v = chunks(q), chunks(k), chunks(v)
    beta = beta.reshape(b, n, c, h).transpose(0, 3, 1, 2)
    gc = jnp.cumsum(g.reshape(b, n, c, h).transpose(0, 3, 1, 2), axis=-1)
    tril = jnp.tril(jnp.ones((c, c), bool))
    strict = jnp.tril(jnp.ones((c, c), bool), -1)
    decay = jnp.exp(jnp.where(tril, gc[..., :, None] - gc[..., None, :], -jnp.inf))
    kb = k * beta[..., None]
    vb = v * beta[..., None]
    a = jnp.where(strict, jnp.einsum('bhnid,bhnjd->bhnij', kb, k) * decay, 0.0) + jnp.eye(c, dtype=jnp.float32)
    rhs = jnp.concatenate([vb, kb * jnp.exp(gc)[..., None]], axis=-1)
    sol = lax.linalg.triangular_solve(a, rhs, left_side=True, lower=True, unit_diagonal=True)
    u, w = sol[..., :dv], sol[..., dv:]
    attn = jnp.einsum('bhnid,bhnjd->bhnij', q, k) * decay
    q_dec = q * jnp.exp(gc)[..., None]
    g_last = gc[..., -1:]
    k_tail = k * jnp.exp(g_last - gc)[..., None]

    def step(state, xs):
        u_i, w_i, a_i, qd_i, kt_i, gl_i = xs
        v_new = u_i - jnp.einsum('bhcd,bhde->bhce', w_i, state)
        o_i = jnp.einsum('bhcd,bhde->bhce', qd_i, state) + jnp.einsum('bhcj,bhje->bhce', a_i, v_new)
        state = state * jnp.exp(gl_i)[..., None] + jnp.einsum('bhcd,bhce->bhde', kt_i, v_new)
        return state, o_i

    xs = tuple(jnp.moveaxis(t, 2, 0) for t in (u, w, attn, q_dec, k_tail, g_last))
    state0 = jnp.zeros((b, h, dk, dv), jnp.float32)
    _, o = lax.scan(step, state0, xs)
    return o.transpose(1, 0, 3, 2, 4).reshape(b, s, h, dv)

def mixer_mla_gdn(h, cos, sin, w_in, q_norm, w_q_b, kv_norm, w_kv_b, qk_norm_q, qk_norm_k,
                  conv_w, a_log, dt_bias, out_norm, w_out):
    b, s, _ = h.shape
    idx = [int(i) for i in np.cumsum(AB_WIDTHS)[:-1]]
    c_q, c_kv, k_r, qkv, z, b_logit, a_logit = jnp.split(h @ w_in, idx, axis=-1)
    q = (rms_norm(c_q, q_norm) @ w_q_b).reshape(b, s, MLA_HEADS, MLA_QK)
    kv = (rms_norm(c_kv, kv_norm) @ w_kv_b).reshape(b, s, MLA_HEADS, MLA_NOPE + MLA_V)
    k_nope, v = kv[..., :MLA_NOPE], kv[..., MLA_NOPE:]
    k = jnp.concatenate([k_nope, jnp.broadcast_to(k_r[:, :, None, :], (b, s, MLA_HEADS, MLA_ROPE))], axis=-1)
    q = apply_rope(rms_norm(q, qk_norm_q), cos, sin)
    k = apply_rope(rms_norm(k, qk_norm_k), cos, sin)
    y_mla = causal_block_attention(q, k, v)
    qkv = jax.nn.silu(causal_short_conv(qkv, conv_w)).astype(jnp.float32)
    gq, gk, gv = jnp.split(qkv, [GDN_HEADS * GDN_DK, 2 * GDN_HEADS * GDN_DK], axis=-1)
    gq = l2_norm(gq.reshape(b, s, GDN_HEADS, GDN_DK)) * (GDN_DK ** -0.5)
    gk = l2_norm(gk.reshape(b, s, GDN_HEADS, GDN_DK))
    gv = gv.reshape(b, s, GDN_HEADS, GDN_DV)
    beta = jax.nn.sigmoid(b_logit.astype(jnp.float32))
    g = -jnp.exp(a_log.astype(jnp.float32)) * jax.nn.softplus(a_logit.astype(jnp.float32) + dt_bias.astype(jnp.float32))
    o = gated_delta_rule(gq, gk, gv, beta, g).astype(h.dtype)
    o = rms_norm(o, out_norm) * jax.nn.silu(z.reshape(b, s, GDN_HEADS, GDN_DV))
    y = jnp.concatenate([y_mla, o.reshape(b, s, GDN_HEADS * GDN_DV)], axis=-1)
    return y @ w_out

def mixer_spatial_gating(h, w_in, v_norm, w_s, b_s, w_out):
    b, s, _ = h.shape
    n = s // SG_CHUNK
    cg = SG_WIDTH // SG_GROUPS
    u, v = jnp.split(jax.nn.gelu(h @ w_in, approximate=False), 2, axis=-1)
    v = rms_norm(v.reshape(b, n, SG_CHUNK, SG_GROUPS, cg), v_norm.reshape(SG_GROUPS, cg))
    w_causal = jnp.where(jnp.tril(jnp.ones((SG_CHUNK, SG_CHUNK), bool)), w_s, 0)
    gate = jnp.einsum('gij,bnjgc->bnigc', w_causal, v) + b_s.T[:, :, None]
    return (u * gate.reshape(b, s, SG_WIDTH)) @ w_out

def setup_inputs(seed: int = 0) -> dict:
    key = jax.random.key(seed)
    ks = jax.random.split(key, 24)
    ne = (DEPTH + 1) // 2
    no = DEPTH // 2
    f32 = jnp.float32

    def nrm(k, shape, fan_in):
        return jax.random.normal(k, shape, f32) * (fan_in ** -0.5)

    def gain(k, shape, sd=0.05):
        return 1.0 + sd * jax.random.normal(k, shape, f32)

    dt = jnp.exp(jax.random.uniform(ks[15], (ne, GDN_HEADS), f32, np.log(0.001), np.log(0.1)))
    return {
        "x": jax.random.normal(ks[0], (BATCH, SEQ, D_MODEL), f32),
        "positions": (jnp.arange(SEQ, dtype=jnp.int32)[None, :]
                      + jax.random.randint(ks[1], (BATCH, 1), 0, 1024, jnp.int32)),
        "norm_w": gain(ks[2], (DEPTH, 3, D_MODEL)),
        "ffn_w_gate": nrm(ks[3], (DEPTH, 2, D_MODEL, D_FF), D_MODEL),
        "ffn_w_up": nrm(ks[4], (DEPTH, 2, D_MODEL, D_FF), D_MODEL),
        "ffn_w_down": nrm(ks[5], (DEPTH, 2, D_FF, D_MODEL), D_FF),
        "ab_w_in": nrm(ks[6], (ne, D_MODEL, IN_AB), D_MODEL),
        "mla_q_norm": gain(ks[7], (ne, MLA_Q_LORA)),
        "mla_w_q_b": nrm(ks[8], (ne, MLA_Q_LORA, MLA_HEADS * MLA_QK), MLA_Q_LORA),
        "mla_kv_norm": gain(ks[9], (ne, MLA_KV_LORA)),
        "mla_w_kv_b": nrm(ks[10], (ne, MLA_KV_LORA, MLA_HEADS * (MLA_NOPE + MLA_V)), MLA_KV_LORA),
        "mla_qk_norm_q": gain(ks[11], (ne, MLA_QK)),
        "mla_qk_norm_k": gain(ks[12], (ne, MLA_QK)),
        "gdn_conv_w": nrm(ks[13], (ne, GDN_CONV, GDN_QKV_W), GDN_CONV),
        "gdn_a_log": jnp.log(jax.random.uniform(ks[14], (ne, GDN_HEADS), f32, 1.0, 16.0)),
        "gdn_dt_bias": jnp.log(jnp.expm1(dt)),
        "gdn_out_norm": gain(ks[16], (ne, GDN_DV)),
        "ab_w_out": nrm(ks[17], (ne, MIX_AB, D_MODEL), MIX_AB),
        "sg_w_in": nrm(ks[18], (no, D_MODEL, 2 * SG_WIDTH), D_MODEL),
        "sg_v_norm": gain(ks[19], (no, SG_WIDTH)),
        "sg_w_s": nrm(ks[20], (no, SG_GROUPS, SG_CHUNK, SG_CHUNK), SG_CHUNK),
        "sg_b_s": gain(ks[21], (no, SG_GROUPS, SG_CHUNK), 0.1),
        "sg_w_out": nrm(ks[22], (no, SG_WIDTH, D_MODEL), SG_WIDTH),
    }

def reference(x, positions, norm_w, ffn_w_gate, ffn_w_up, ffn_w_down, ab_w_in, mla_q_norm, mla_w_q_b,
              mla_kv_norm, mla_w_kv_b, mla_qk_norm_q, mla_qk_norm_k, gdn_conv_w, gdn_a_log, gdn_dt_bias,
              gdn_out_norm, ab_w_out, sg_w_in, sg_v_norm, sg_w_s, sg_b_s, sg_w_out):
    cos, sin = rope_tables(positions)
    for l in range(DEPTH):
        i = l // 2
        x = x + 0.5 * swiglu(rms_norm(x, norm_w[l, 0]), ffn_w_gate[l, 0], ffn_w_up[l, 0], ffn_w_down[l, 0])
        h = rms_norm(x, norm_w[l, 1])
        if l % 2 == 0:
            x = x + mixer_mla_gdn(h, cos, sin, ab_w_in[i], mla_q_norm[i], mla_w_q_b[i], mla_kv_norm[i],
                                  mla_w_kv_b[i], mla_qk_norm_q[i], mla_qk_norm_k[i], gdn_conv_w[i],
                                  gdn_a_log[i], gdn_dt_bias[i], gdn_out_norm[i], ab_w_out[i])
        else:
            x = x + mixer_spatial_gating(h, sg_w_in[i], sg_v_norm[i], sg_w_s[i], sg_b_s[i], sg_w_out[i])
        x = x + 0.5 * swiglu(rms_norm(x, norm_w[l, 2]), ffn_w_gate[l, 1], ffn_w_up[l, 1], ffn_w_down[l, 1])
    return x


_drawn_inputs = setup_inputs


def setup_inputs(seed=0):
    import zlib

    import numpy as np

    out = dict(_drawn_inputs(seed))
    spreads = {}
    factors = {'mla_q_norm': 8.0,
     'mla_kv_norm': 4.805,
     'mla_qk_norm_q': 8.0,
     'mla_qk_norm_k': 8.0,
     'sg_v_norm': 9.916,
     'gdn_out_norm': 7.187,
     'sg_b_s': 3.335}
    for name, (base, spread) in spreads.items():
        noise = np.random.default_rng([zlib.crc32(name.encode()), seed]).standard_normal(out[name].shape)
        drawn = base * np.exp(spread * noise) if base else spread * noise
        out[name] = __import__('jax').numpy.asarray(drawn.astype(out[name].dtype))
    for name, factor in factors.items():
        out[name] = (out[name] * factor).astype(out[name].dtype)
    return out
```

```python
import numpy as np
import concourse.bass as bass
from concourse import mybir
from contextlib import ExitStack

P = 128
D_MODEL, SEQ, D_FF = 1024, 256, 2816
NT = SEQ // P
KD = D_MODEL // P
KF = D_FF // P
Q_LORA, KV_LORA, NOPE, ROPE, VDIM = 256, 128, 64, 32, 64
QK = NOPE + ROPE
HALF = ROPE // 2
HEADS = 8
DK = 64
CHUNK = 64
CONV = 4
PAIRS = HEADS // 2
AB_W = Q_LORA + KV_LORA + ROPE
QKV0 = AB_W
Z0 = QKV0 + 3 * HEADS * DK
BA0 = Z0 + HEADS * DK
AW = AB_W + 2 * HEADS
SGW, GROUPS, CG = 2048, 8, 256
EPS = 1e-6
SLOT = 2048
SLOTS = 4
LEVELS = (1, 2, 4, 8, 16, 32)


def constants():
    p = np.arange(P)[:, None]
    i64, i128 = np.arange(64)[None, :], np.arange(P)[None, :]
    q = p % 64
    parts = [
        ("ident", i128 == p),
        ("cumul", q <= i64),
        ("ones", np.ones((P, 64))),
        ("causal", i64 <= q),
        ("eye64", i64 == q),
        ("first", (q // 2 == i64 // 2) & (q % 2 == 1) & (i64 % 2 == 0)),
    ]
    for b in LEVELS:
        up = (q // (2 * b) == i64 // (2 * b)) & ((i64 // b) % 2 == 1) & ((q // b) % 2 == 0)
        parts.append((f"level{b}", up))
    parts.append(("future", np.where(i128 <= p, 0.0, -3.0e38)))
    parts.append(("tril128", i128 <= p))
    freq = np.float32(10000.0) ** (-np.arange(0, ROPE, 2, dtype=np.float32) / np.float32(ROPE))
    parts.append(("freq", np.broadcast_to(freq, (P, HALF))))
    at, where = 0, {}
    for name, a in parts:
        where[name] = (at, a.shape[1])
        at += a.shape[1]
    return np.ascontiguousarray(np.concatenate([a.astype(np.float32) for _, a in parts], axis=1)), where


def build_trunk(nc, x, positions, norm_w, w_gate, w_up, w_down, ab_in, q_norm, w_q_b, kv_norm, w_kv_b,
                qk_norm_q, qk_norm_k, conv_w, a_log, dt_bias, gdn_norm, ab_out, sg_in, sg_norm, sg_ws,
                sg_bs, sg_out, const_dram, out, stop_after=None):
    f32, f32r, i32 = mybir.dt.float32, mybir.dt.float32r, mybir.dt.int32
    ALU, ACT, AX = mybir.AluOpType, mybir.ActivationFunctionType, mybir.AxisListType
    const_at = constants()[1]
    n_const = const_dram.shape[1]
    ds = bass.ds

    def rows(w, k0, kt, c0, cw):
        return w[k0 * P:(k0 + kt) * P, :].rearrange("(k p) n -> p k n", p=P)[:, :, c0:c0 + cw]

    units = []

    def unit(kt, width, *pieces):
        units.append((kt, width, pieces))
        return len(units) - 1

    def ffn_units(l, s):
        g, u, d = w_gate[l, s], w_up[l, s], w_down[l, s]
        base = len(units)
        for c in range(5):
            for w in (g, u):
                for k0 in (0, 4):
                    unit(4, 512, (0, rows(w, k0, 4, 512 * c, 512)))
        for w in (g, u):
            unit(8, 256, (0, rows(w, 0, 8, 2560, 256)))
        for k in range(KF // 2):
            unit(2, 1024, (0, rows(d, 2 * k, 2, 0, 1024)))
        return base

    def ab_units():
        w = ab_in[0]
        base = len(units)
        for k0 in (0, 4):
            unit(4, AW, (0, rows(w, k0, 4, 0, AB_W)), (AB_W, rows(w, k0, 4, BA0, 2 * HEADS)))
        for c in (0, 1):
            unit(8, 256, (0, rows(w, 0, 8, QKV0 + 256 * c, 256)))
        unit(2, 768, (0, rows(w_q_b[0], 0, 2, 0, 768)))
        unit(1, 1024, (0, rows(w_kv_b[0], 0, 1, 0, 1024)))
        for c in range(2, 6):
            unit(8, 256, (0, rows(w, 0, 8, QKV0 + 256 * c, 256)))
        for k0 in (0, 4):
            unit(4, 512, (0, rows(w, k0, 4, Z0, 512)))
        for k in range(4):
            unit(2, 1024, (0, rows(ab_out[0], 2 * k, 2, 0, 1024)))
        return base

    def sg_units():
        base = len(units)
        for c in (4, 5, 6, 7, 0, 1, 2, 3):
            for k0 in (0, 4):
                unit(4, 512, (0, rows(sg_in[0], k0, 4, 512 * c, 512)))
        for k in range(8):
            unit(2, 1024, (0, rows(sg_out[0], 2 * k, 2, 0, 1024)))
        return base

    u_ffn = [0] * 4
    u_ffn[0] = ffn_units(0, 0)
    u_ab = ab_units()
    u_ffn[1] = ffn_units(0, 1)
    u_ffn[2] = ffn_units(1, 0)
    u_sg = sg_units()
    u_ffn[3] = ffn_units(1, 1)
    N_UNITS = len(units)
    arrivals, per_slot = [], [0] * SLOTS
    for j, (_, _, pieces) in enumerate(units):
        per_slot[j % SLOTS] += len(pieces)
        arrivals.append(per_slot[j % SLOTS])

    N_ROWS = 107

    ctx = ExitStack()
    with ctx:
        def sb(name, shape, dt=f32):
            return ctx.enter_context(nc.sbuf_tensor(name, shape, dt))

        sems = {}

        def S(name):
            if name not in sems:
                sems[name] = ctx.enter_context(nc.semaphore(name))
            return sems[name]

        X = sb("X", [P, NT, D_MODEL])
        C = sb("C", [P, n_const])
        param_rows = sb("param_rows", [N_ROWS, P])
        param_cols = sb("param_cols", [P, N_ROWS])
        pos_rows = sb("pos_rows", [NT, 2, P])
        raw = sb("raw", [P, SLOTS, SLOT])
        whi = sb("whi", [P, SLOTS, SLOT], f32r)
        wlo = sb("wlo", [P, SLOTS, SLOT], f32r)
        small = sb("small", [P, 720])
        with ExitStack() as over:
            hTh = over.enter_context(nc.sbuf_tensor("hTh", [P, KF, SEQ], f32r))
            hTl = over.enter_context(nc.sbuf_tensor("hTl", [P, KF, SEQ], f32r))
            xTh = over.enter_context(nc.sbuf_tensor("xTh", [P, KD, SEQ], f32r))
            xTl = over.enter_context(nc.sbuf_tensor("xTl", [P, KD, SEQ], f32r))
        H1 = KF * SEQ
        XT0 = 2 * H1
        R0 = XT0 + 2 * KD * SEQ
        arena = sb("arena", [P, R0 + 8544])

        def at(off, *dims):
            n = int(np.prod(dims))
            v = arena[:, off:off + n]
            if len(dims) == 2:
                v = v.rearrange("p (a b) -> p a b", b=dims[1])
            if len(dims) == 3:
                v = v.rearrange("p (a b c) -> p a b c", b=dims[1], c=dims[2])
            return v

        cursor = [0]

        def tiny(*dims):
            n = int(np.prod(dims))
            v = small[:, cursor[0]:cursor[0] + n]
            cursor[0] += n
            if len(dims) == 2:
                v = v.rearrange("p (a b) -> p a b", b=dims[1])
            if len(dims) == 3:
                v = v.rearrange("p (a b c) -> p a b c", b=dims[1], c=dims[2])
            return v

        def const(name):
            o, n = const_at[name]
            return C[:, o:o + n]

        normT = param_cols[:, 0:48].rearrange("p (s k) -> p s k", k=KD)
        convT = param_cols[:, 48:96].rearrange("p (j b) -> p b j", j=CONV)
        qn_col, kvn_col = param_cols[:, 96:98], param_cols[:, 98:99]
        bsT = param_cols[:, 99:107]
        ident, cumul, ones64 = const("ident"), const("cumul"), const("ones")

        s_buf = at(R0, NT, 512)
        h_buf = at(R0 + 1024, NT, 512)
        squares = [at(R0, 1024), at(R0 + 1024, 1024)]
        wsT = at(4096, GROUPS, P)
        V = at(R0 + 4096, NT, SGW)
        v_norm_row = at(R0 + 2048, SGW)
        ws_raw = at(0, GROUPS, P)
        xs = at(0, NT, D_MODEL)
        qTm, kTm = at(0, HEADS, SEQ), at(2048, HEADS, SEQ)
        tmp = at(4096, 1536)
        scores = at(H1, 3, P)
        probs = at(H1 + 384, 3, P)
        qm = at(6400, NT, HEADS * QK)
        kvm = at(7936, NT, HEADS * 128)
        pT = at(9984, 2, 3 * P)
        km = at(R0, NT, HEADS * QK)
        PM = at(R0 + 1536, NT, AW)
        Y = at(R0 + 2400, NT, D_MODEL)
        SZ = at(R0 + 4448, NT, 512)
        QKVn = [at(R0 + 5472 + 1024 * i, NT, 512) for i in range(3)]
        yc = at(2048, 2, 2, SEQ)
        (gU, Dec, DecB, Lm, Am, LT, AT, Dm, DT, kbe, kt) = [at(1024 * i, 1024) for i in range(11)]
        M1, Loff = gU, [Dec, Am]
        kT, qT, qdT, wT = [at(XT0 + 1024 * i, PAIRS, SEQ) for i in range(4)]
        qd = at(R0, NT, 512)
        state = at(R0 + 1024, PAIRS, P)
        v_new = at(3072, 512)
        s_dec = at(3584, PAIRS, P)

        sumsq, rstd = tiny(2), tiny(2)
        rs_a, rs_t, rs_y = tiny(16), tiny(16), tiny(16)
        c_ss, c_rs = tiny(4), tiny(4)
        head_ss = tiny(16)
        qkn_q, qkn_k, gdn_w = tiny(QK), tiny(QK), tiny(DK)
        cosT, sinT, ang, angk = tiny(NT, HALF), tiny(NT, HALF), tiny(NT, HALF), tiny(NT, HALF)
        pos_f = tiny(NT)
        alog, dtb = tiny(HEADS), tiny(HEADS)
        beta, gdec, gc, egc, begc, ek, sp = [tiny(NT, HEADS) for _ in range(7)]
        eg = tiny(4, PAIRS)
        smax, nbias, row_sum, rden = tiny(3), tiny(2), tiny(NT, HEADS), tiny(NT, HEADS)
        v_ss = tiny(4)

        B = [ctx.enter_context(nc.psum_tensor(f"B{i}", [P, 512], f32)) for i in range(8)]

        def bc(ap, shape):
            return ap.broadcast_to(shape)

        def unit_view(ring, j, kt, width):
            return ring[:, j % SLOTS, 0:kt * width].rearrange("p (k n) -> p k n", n=width)

        X_BANK = [4, 5, 2, 3]
        N_LIVE = {"ffn0": 33, "ab": u_ffn[1]}.get(stop_after, N_UNITS)
        FFN_SUB = [0, 2, 3, 5]
        HT_FREE = 2
        D_BANK = ((6, 7), (0, 1))
        N_SMALL = 5
        C_UNIT = [u_ab + i for i in (2, 3, 6, 7, 8, 9)]
        XT = [0, 1, 3, 4, 5, 6]
        HT = {0: 0, 2: 11, 3: 22, 4: 33, 5: 41}

        block = ctx.enter_context(nc.Block())

        @block.sync
        def _(sp_):
            def load(dst, src, name):
                sp_.dma_start(dst, src).then_inc(S(name), 16)

            load(X[:], x[0].rearrange("(t p) d -> p t d", p=P), "x_loaded")
            load(C[:], const_dram, "const_loaded")

            def load_unit(j, shift=None):
                kt, width, pieces = units[j]
                turn = 0 if shift is None else shift[0]
                if j >= SLOTS:
                    sp_.wait_ge(S("lo_ready"), turn * SLOTS + (j - SLOTS + 1))
                for c0, src in (pieces if shift is None else [(0, shift[1])]):
                    dst = unit_view(raw, j, kt, width)[:, :, c0:c0 + src.shape[2]]
                    sp_.dma_start(dst, src).then_inc(S(f"raw_loaded{j % SLOTS}"), 16)

            def ffn_loads(base, l, s):
                for j in range(base, base + 4):
                    load_unit(j)
                with sp_.Fori(0, 4) as turn:
                    i = 4
                    for w in (w_gate, w_up):
                        for k0 in (0, 4):
                            src = w[l, s, k0 * P:(k0 + 4) * P, :].rearrange("(k p) n -> p k n", p=P)
                            load_unit(base + i, (turn, src[:, :, ds(turn * 512 + 512, 512)]))
                            i += 1
                for j in range(base + 20, base + 33):
                    load_unit(j)

            ffn_loads(u_ffn[0], 0, 0)
            if stop_after == "ffn0":
                pass
            else:
                for j in range(u_ab, u_ab + 16):
                    load_unit(j)
            if stop_after not in ("ffn0", "ab"):
                ffn_loads(u_ffn[1], 0, 1)
                ffn_loads(u_ffn[2], 1, 0)
                for j in range(u_sg, u_sg + 24):
                    load_unit(j)
                ffn_loads(u_ffn[3], 1, 1)
            n_x = {"ffn0": 1, "ab": 2}.get(stop_after, 6)
            for t in range(NT):
                sp_.wait_ge(S("x_updated"), 4 * (n_x - 1) + 2 * (t + 1))
                sp_.dma_start(out[0, t * P:(t + 1) * P, :], X[:, t, :]).then_inc(S("out_stored"), 16)
            sp_.wait_ge(S("out_stored"), 32)

        @block.gpsimd
        def _(pool):
            def load(dst, src, name):
                pool.dma_start(dst, src).then_inc(S(name), 16)

            if stop_after == "ffn0":
                return
            for dst, src, n in ((qkn_q, qk_norm_q, QK), (qkn_k, qk_norm_k, QK), (gdn_w, gdn_norm, DK),
                                (alog, a_log, HEADS), (dtb, dt_bias, HEADS)):
                load(dst, bc(src, [P, n]), "small_loaded")

            k4 = km.rearrange("p t (h d) -> p t h d", d=QK)
            kv4 = kvm.rearrange("p t (h d) -> p t h d", d=128)
            pool.wait_ge(S("kv_out"), 4)
            for t in range(NT):
                nc.gpsimd.tensor_copy(k4[:, t, :, 0:NOPE], kv4[:, t, :, 0:NOPE]).then_inc(S("k_built"), 1)
                nc.gpsimd.tensor_copy(k4[:, t, :, NOPE:QK],
                                      bc(PM[:, t:t + 1, Q_LORA + KV_LORA:AB_W], [P, HEADS, ROPE])
                                      ).then_inc(S("k_built"), 1)
            pool.wait_ge(S("z_out"), 2)
            pool.wait_ge(S("small_loaded"), 16 * N_SMALL)
            z4 = SZ.rearrange("p t (h d) -> p (t h) d", d=DK)
            nc.gpsimd.tensor_tensor(z4, z4, bc(gdn_w.unsqueeze(1), [P, NT * HEADS, DK]), ALU.mult
                                    ).then_inc(S("z_weighted"), 1)
            pool.wait_ge(S("lt_ready"), 4)
            for n, b in enumerate(LEVELS[1:]):
                if n == 1:
                    pool.wait_ge(S("at_ready"), 4)
                if n >= 2:
                    pool.wait_ge(S("m1_sums"), 4 * (n - 1))
                mask = bc(const(f"level{b}").unsqueeze(1), [P, 16, 64])
                nc.gpsimd.tensor_tensor(Loff[n % 2].rearrange("p (m i) -> p m i", i=64),
                                        LT.rearrange("p (m i) -> p m i", i=64), mask, ALU.mult
                                        ).then_inc(S("loff_ready"), 1)
            if stop_after == "ab":
                return
            pool.wait_ge(S("x_updated"), 8)
            load(v_norm_row, bc(sg_norm, [P, SGW]), "sg_loaded")
            pool.wait_ge(S("x_updated"), 16)
            load(ws_raw, sg_ws[0].rearrange("g i j -> i g j"), "sg_loaded")
            pool.wait_ge(S("sg_loaded"), 32)
            nc.gpsimd.tensor_tensor(ws_raw, ws_raw, bc(const("tril128").unsqueeze(1), [P, GROUPS, P]),
                                    ALU.mult).then_inc(S("ws_masked"), 1)
            for c in range(4):
                pool.wait_ge(S("v_scaled"), c + 1)
                nc.gpsimd.tensor_tensor(V[:, :, 512 * c:512 * c + 512], V[:, :, 512 * c:512 * c + 512],
                                        bc(v_norm_row[:, 512 * c:512 * c + 512].unsqueeze(1), [P, NT, 512]),
                                        ALU.mult).then_inc(S("v_ready"), 1)

        @block.scalar
        def _(act):
            A = nc.scalar.activation

            def hi(j, turn=0):
                if j >= N_LIVE:
                    return
                kt, width, _ = units[j]
                act.wait_ge(S(f"raw_loaded{j % SLOTS}"), turn * 16 + 16 * arrivals[j])
                if j >= SLOTS:
                    act.wait_ge(S("unit_done"), turn * SLOTS + (j - SLOTS + 1))
                A(whi[:, j % SLOTS, 0:kt * width], raw[:, j % SLOTS, 0:kt * width], ACT.Copy
                  ).then_inc(S("hi_ready"), 1)

            def x_hi(xi, norm=None):
                for k in range(KD):
                    act.wait_ge(S("xT_sums"), 4 * xi + k // 2 + 1)
                    A(xTh[:, k, :], B[X_BANK[k // 2]][:, 256 * (k % 2):256 * (k % 2) + 256], ACT.Copy,
                      scale=1.0 if norm is None else normT[:, norm, k:k + 1]).then_inc(S("xT_hi"), 1)

            def x_squares(s):
                for t in range(NT):
                    if s > 0:
                        act.wait_ge(S("x_updated"), 4 * (s - 1) + 2 * (t + 1))
                    A(squares[t], X[:, t, :], ACT.Square, accum_out=sumsq[:, t:t + 1]).then_inc(S("x_squared"), 1)

            def hT_hi(done, k0, n_blocks, turn=None):
                for b in range(0, n_blocks, 2):
                    act.wait_ge(S("hT_sums"), (0 if turn is None else turn * 2) + (done + b // 2 + 1))
                    dst = hTh[:, k0 + b:k0 + b + 2, :] if turn is None else hTh[:, ds(turn * 4 + b, 2), :]
                    A(dst, B[4 + b // 2][:].rearrange("p (b n) -> p b n", n=SEQ), ACT.Copy
                      ).then_inc(S("hT_hi"), 1)

            def silu_gate(f, c, width, turn=0):
                act.wait_ge(S("unit_done"), turn * SLOTS + u_ffn[f] + (4 * c + 2 if c < 5 else 21))
                if c == 0:
                    act.wait_ge(S("rstd_ready"), FFN_SUB[f] + 1)
                else:
                    act.wait_ge(S("h_ready"), turn * 2 + (12 * f + 2 * c))
                for t in range(NT):
                    A(s_buf[:, t, 0:width], B[t][:, 0:width], ACT.Silu, scale=rstd[:, t:t + 1]
                      ).then_inc(S("silu_done"), 1)

            def ffn(f):
                s, base = FFN_SUB[f], u_ffn[f]
                x_hi(XT[s], s)
                hi(base + 3)
                x_squares(s)
                hi(base + 4)
                silu_gate(f, 0, 512)
                for j in (5, 6, 7):
                    hi(base + j)
                with act.Fori(0, 4) as turn:
                    hi(base + 8, turn)
                    silu_gate(f, 1, 512, turn)
                    hi(base + 9, turn)
                    hT_hi(HT[s], 0, 4, turn)
                    hi(base + 10, turn)
                    hi(base + 11, turn)
                silu_gate(f, 5, 256)
                hi(base + 24)
                hT_hi(HT[s] + 8, 16, 4)
                hi(base + 25)
                hT_hi(HT[s] + 10, 20, 2)
                for j in range(26, 36):
                    hi(base + j)

            for r0, src in ((0, norm_w.rearrange("l s (k p) -> (l s k) p", p=P)),
                            (48, conv_w[0].rearrange("j (b p) -> (j b) p", p=P)),
                            (96, q_norm[0].rearrange("(b p) -> b p", p=P)),
                            (98, kv_norm), (99, sg_bs[0])):
                act.dma_start(param_rows[r0:r0 + src.shape[0], :], src).then_inc(S("rows_loaded"), 16)
            act.dma_start(pos_rows[:, 0, :].bitcast(i32), positions[0].rearrange("(t p) -> t p", p=P)
                          ).then_inc(S("pos_loaded"), 16)
            for j in range(3):
                hi(j)
            act.wait_ge(S("param_sums"), 1)
            A(param_cols[:], B[7][:, 0:N_ROWS], ACT.Copy).then_inc(S("params_ready"), 1)
            act.wait_ge(S("params_ready"), 1)
            act.wait_ge(S("x_loaded"), 16)
            ffn(0)
            if stop_after == "ffn0":
                return

            b = u_ab
            x_squares(1)
            act.wait_ge(S("small_loaded"), 16 * N_SMALL)
            x_hi(XT[1], 1)
            hi(b + 3)
            act.wait_ge(S("unit_done"), b + 2)
            for t in range(NT):
                A(PM[:, t, :], B[t][:, 0:AW], ACT.Copy).then_inc(S("pm_out"), 1)
            hi(b + 4)
            hi(b + 5)

            def tap(i):
                act.wait_ge(S("unit_done"), C_UNIT[i] + 1)
                if i >= 2:
                    act.wait_ge(S("nt_sums"), i - 1)
                for s in range(2):
                    A(yc[:, i % 2, s, :], B[2 + i % 2][:, 256 * s:256 * s + 256], ACT.Copy,
                      scale=convT[:, 2 * i + s, CONV - 1:CONV]).then_inc(S("tap_done"), 1)

            def conv_silu(i):
                act.wait_ge(S("conv_done"), 2 * i + 2)
                A(yc[:, i % 2, :, :], yc[:, i % 2, :, :], ACT.Silu).then_inc(S("yc_ready"), 1)

            def nt_out(i):
                act.wait_ge(S("nt_sums"), i + 1)
                A(QKVn[i // 2][:, :, 256 * (i % 2):256 * (i % 2) + 256],
                  B[5][:].rearrange("p (t c) -> p t c", t=NT), ACT.Copy).then_inc(S("nt_out"), 1)

            tap(0)
            hi(b + 6)
            tap(1)
            conv_silu(0)
            hi(b + 7)
            act.wait_ge(S("cT_sums"), 1)
            for k in range(3):
                if k == 2:
                    act.wait_ge(S("cT_sums"), 2)
                A(hTh[:, k, :], (B[4][:, 256 * k:256 * k + 256] if k < 2 else B[5][:, 0:256]), ACT.Copy,
                  scale=(qn_col[:, k:k + 1] if k < 2 else kvn_col)).then_inc(S("cT_hi"), 1)
            conv_silu(1)
            act.wait_ge(S("unit_done"), b + 5)
            for t in range(NT):
                q0, q1 = (B[6], B[7]) if t == 0 else (B[0], B[1])
                A(qm[:, t, 0:512], q0[:], ACT.Copy).then_inc(S("q_out"), 1)
                A(qm[:, t, 512:768], q1[:, 0:256], ACT.Copy).then_inc(S("q_out"), 1)
            for t in range(NT):
                act.wait_ge(*((S("kv_sums"), 1) if t == 0 else (S("unit_done"), b + 6)))
                q0, q1 = (B[4], B[5]) if t == 0 else (B[6], B[7])
                A(kvm[:, t, 0:512], q0[:], ACT.Copy).then_inc(S("kv_out"), 1)
                A(kvm[:, t, 512:1024], q1[:], ACT.Copy).then_inc(S("kv_out"), 1)
            hi(b + 8)
            hi(b + 9)
            for i in range(2, 6):
                tap(i)
                nt_out(i - 2)
                conv_silu(i)
                hi(b + 8 + i)
            act.wait_ge(S("unit_done"), b + 12)
            for t in range(NT):
                A(SZ[:, t, :], B[t][:], ACT.Silu).then_inc(S("z_out"), 1)
            hi(b + 14)
            hi(b + 15)
            nt_out(4)
            nt_out(5)
            act.wait_ge(S("angles"), 1)
            A(sinT, ang, ACT.Sin).then_inc(S("sines"), 1)
            A(cosT, ang, ACT.Sin, scale=0.5).then_inc(S("sines"), 1)
            act.wait_ge(S("a_abs"), 1)
            A(beta, PM[:, :, AB_W:AB_W + HEADS], ACT.Exp, scale=-1.0).then_inc(S("gate_exps"), 1)
            A(gc, egc, ACT.Exp, scale=-1.0).then_inc(S("gate_exps"), 1)
            A(alog, alog, ACT.Exp).then_inc(S("gate_exps"), 1)
            act.wait_ge(S("gate_exps"), 3)
            A(gc, gc, ACT.Ln, bias=1.0).then_inc(S("gate_ln"), 1)

            def qkT_out(i):
                act.wait_ge(S("qkT_sums"), i + 1)
                dst, t, g = (qTm, kTm)[i // 4], i // 2 % 2, i % 2
                A(dst[0:QK, 4 * g:4 * g + 4, P * t:P * t + P],
                  B[(4, 6)[i % 2]][0:QK, :].rearrange("p (h n) -> p h n", n=P), ACT.Copy
                  ).then_inc(S("qkT_out"), 1)

            for i in range(8):
                qkT_out(i)
            scale = float(QK) ** -0.5
            for h in range(HEADS):
                act.wait_ge(S("softmax_in"), h + 1)
                if h:
                    act.wait_ge(S("pT_sums"), h)
                A(probs[:, 0, :], scores[:, 0, :], ACT.Exp, scale=scale, bias=nbias[:, 0:1],
                  accum_out=row_sum[:, 0, h:h + 1]).then_inc(S("exp_done"), 1)
                A(probs[:, 1:3, :], scores[:, 1:3, :], ACT.Exp, scale=scale, bias=nbias[:, 1:2],
                  accum_out=row_sum[:, 1, h:h + 1]).then_inc(S("exp_done"), 1)
                if h >= 2:
                    act.wait_ge(S("pv_sums"), h - 1)
                act.wait_ge(S("pT_sums"), h + 1)
                A(pT[:, h % 2, :], B[4][:, 0:3 * P], ACT.Copy).then_inc(S("pT_out"), 1)

            act.wait_ge(S("gc_ready"), 1)
            for c in range(2):
                for odd in range(2):
                    r = slice(64 * odd, 64 * odd + 64)
                    src = B[2 + c][r, 32:48].rearrange("p (t q o) -> p t q o", t=NT, o=2)[:, :, :, odd]
                    dst = eg[r].rearrange("p (t c) q -> p t c q", c=2)[:, :, c, :]
                    A(dst, src, ACT.Exp).then_inc(S("eg_ready"), 1)
            A(egc, gc, ACT.Exp).then_inc(S("decay_exps"), 1)
            A(ek, ek, ACT.Exp).then_inc(S("decay_exps"), 1)
            act.wait_ge(S("dec_diff"), 1)
            A(Dec, Dec, ACT.Exp, scale=-1.0).then_inc(S("dec_exp"), 1)

            for i in range(6):
                act.wait_ge(S("dT_sums"), i + 1)
                A((qT, kT, qdT)[i // 2][:, 2 * (i % 2):2 * (i % 2) + 2, :],
                  B[i % 2][:].rearrange("p (q n) -> p q n", n=SEQ), ACT.Copy).then_inc(S("dT_out"), 1)
            for n, dst in enumerate((LT, AT)):
                for t in range(NT):
                    for c in range(2):
                        r = slice(64 * c, 64 * c + 64)
                        act.wait_ge(S("la_sums"), 4 * n + 2 * t + c + 1)
                        A(dst[r, 512 * t:512 * t + 512], B[4 * n + 2 * t + c][r, :], ACT.Copy
                          ).then_inc(S("lt_ready") if n == 0 else S("at_ready"), 1)
            for n in range(5):
                for t in range(NT):
                    for c in range(2):
                        r = slice(64 * c, 64 * c + 64)
                        act.wait_ge(S("m1_sums"), 4 * n + 2 * t + c + 1)
                        A(M1[r, 512 * t:512 * t + 512], B[4 * (n % 2) + 2 * t + c][r, :], ACT.Copy
                          ).then_inc(S("m1_ready"), 1)
            for c in range(2):
                act.wait_ge(S("w_sums"), c + 1)
                dst = wT.rearrange("p q (t c i) -> p t q c i", t=NT, c=2)[:, :, :, c, :]
                A(dst, B[4 + c][:].rearrange("p (t q i) -> p t q i", t=NT, i=64), ACT.Copy, scale=-1.0
                  ).then_inc(S("w_ready"), 1)
            for n in range(4):
                t, c = n // 2, n % 2
                r = slice(64 * c, 64 * c + 64)
                act.wait_ge(S("v_sums"), n + 1)
                A(v_new[r, :], B[0][r, :], ACT.Copy).then_inc(S("v_new_ready"), 1)
                act.wait_ge(S("o_sums"), n + 1)
                A(Y[r, t, 512:1024], B[1][r, :], ACT.Copy).then_inc(S("o_out"), 1)
            x_hi(2)
            for j in range(16, 19):
                hi(b + j)
            if stop_after == "ab":
                return

            ffn(1)
            ffn(2)

            b = u_sg
            x_hi(XT[4], 4)
            hi(b + 3)
            x_squares(4)

            def gate_out(c):
                for t in range(NT):
                    act.wait_ge(S("gate_sums"), 2 * c + t + 1)
                    for g in (2 * c, 2 * c + 1):
                        A(V[:, t, CG * g:CG * g + CG], B[6 + t][:, CG * (g % 2):CG * (g % 2) + CG],
                          ACT.Identity, bias=bsT[:, g:g + 1]).then_inc(S("gate_ready"), 1)

            for c in range(4):
                act.wait_ge(S("unit_done"), b + 2 * c + 2)
                if c == 0:
                    act.wait_ge(S("rstd_ready"), 5)
                for t in range(NT):
                    A(V[:, t, 512 * c:512 * c + 512], B[2 * (c % 2) + t][:], ACT.Gelu, scale=rstd[:, t:t + 1]
                      ).then_inc(S("v_gelu"), 1)
                if c:
                    act.wait_ge(S("v_scaled"), c)
                act.wait_ge(S("v_gelu"), 2 * c + 2)
                for t in range(NT):
                    for g in range(2):
                        A(squares[t][:, CG * g:CG * g + CG], V[:, t, 512 * c + CG * g:512 * c + CG * g + CG],
                          ACT.Square, accum_out=v_ss[:, 2 * t + g:2 * t + g + 1]).then_inc(S("v_squared"), 1)
                hi(b + 2 * c + 4)
                hi(b + 2 * c + 5)
                if c == 0:
                    for n in range(2):
                        act.wait_ge(S("wsT_sums"), n + 1)
                        A(wsT[:, 4 * n:4 * n + 4, :], B[6 + n][:].rearrange("p (g n) -> p g n", n=P), ACT.Copy
                          ).then_inc(S("wsT_ready"), 1)
                else:
                    gate_out(c - 1)
            for c in range(4):
                act.wait_ge(S("unit_done"), b + 8 + 2 * c + 2)
                if c == 0:
                    act.wait_ge(S("v_scaled"), 4)
                else:
                    act.wait_ge(S("y_ready"), c)
                for t in range(NT):
                    A(s_buf[:, t, :], B[2 * (c % 2) + t][:], ACT.Gelu, scale=rstd[:, t:t + 1]
                      ).then_inc(S("u_gelu"), 1)
                if c == 0:
                    gate_out(3)
                hi(b + 8 + 2 * c + 4)
                hi(b + 8 + 2 * c + 5)
                if c >= 1:
                    hT_hi(HT[4] + 2 * (c - 1), 4 * (c - 1), 4)
            hT_hi(HT[4] + 6, 12, 4)
            for j in range(20, 27):
                hi(b + j)
            ffn(3)

        @block.vector
        def _(dve):
            TT, TS, STT = nc.vector.tensor_tensor, nc.vector.tensor_scalar, nc.vector.scalar_tensor_tensor
            links = [0]

            def link(ins):
                links[0] += 1
                ins.then_inc(S("dve_chain"), 1)
                dve.wait_ge(S("dve_chain"), links[0])

            def rsqrt(dst, ss, n, inv, extra=1.0):
                a, u, y = rs_a[:, 0:n], rs_t[:, 0:n], rs_y[:, 0:n]
                link(TS(a, ss, inv, EPS, ALU.mult, ALU.add))
                link(TS(u.bitcast(i32), a.bitcast(i32), 1, None, ALU.logical_shift_right))
                link(TS(y.bitcast(i32), u.bitcast(i32), -1.0, float(0x5F3759DF), ALU.mult, ALU.add))
                for step in range(3):
                    last = step == 2
                    link(TT(u, y, y, ALU.mult))
                    link(TT(u, u, a, ALU.mult))
                    c = extra if last else 1.0
                    link(TS(u, u, -0.5 * c, 1.5 * c, ALU.mult, ALU.add))
                    if not last:
                        link(TT(y, y, u, ALU.mult))
                return TT(dst, y, u, ALU.mult)

            def lo(j, turn=0):
                if j >= N_LIVE:
                    return
                kt, width, _ = units[j]
                dve.wait_ge(S("hi_ready"), turn * SLOTS + (j + 1))
                n = kt * width
                TT(wlo[:, j % SLOTS, 0:n], raw[:, j % SLOTS, 0:n], whi[:, j % SLOTS, 0:n].bitcast(f32),
                   ALU.subtract).then_inc(S("lo_ready"), 1)

            def x_lo(xi, norm=None):
                for k in range(KD):
                    dve.wait_ge(S("xT_hi"), 8 * xi + 2 * (k // 2) + 2)
                    STT(xTl[:, k, :], B[X_BANK[k // 2]][:, 256 * (k % 2):256 * (k % 2) + 256],
                        1.0 if norm is None else normT[:, norm, k:k + 1], xTh[:, k, :].bitcast(f32),
                        ALU.mult, ALU.subtract).then_inc(S("xT_lo"), 1)

            def row_norm(s):
                dve.wait_ge(S("x_squared"), 2 * s + 2)
                rsqrt(rstd, sumsq, 2, 1.0 / D_MODEL).then_inc(S("rstd_ready"), 1)

            def hT_lo(done, k0, n_blocks, turn=None):
                for b in range(0, n_blocks, 2):
                    dve.wait_ge(S("hT_hi"), (0 if turn is None else turn * 2) + (done + b // 2 + 1))
                    if turn is None:
                        dst, top = hTl[:, k0 + b:k0 + b + 2, :], hTh[:, k0 + b:k0 + b + 2, :]
                    else:
                        dst, top = hTl[:, ds(turn * 4 + b, 2), :], hTh[:, ds(turn * 4 + b, 2), :]
                    TT(dst, B[4 + b // 2][:].rearrange("p (b n) -> p b n", n=SEQ), top.bitcast(f32),
                       ALU.subtract).then_inc(S("hT_lo"), 1)

            def up_product(f, c, width, turn=0):
                dve.wait_ge(S("unit_done"), turn * SLOTS + u_ffn[f] + (4 * c + 4 if c < 5 else 22))
                for t in range(NT):
                    dve.wait_ge(S("silu_done"), turn * 2 + (12 * f + 2 * c + t + 1))
                    STT(h_buf[:, t, 0:width], B[2 + t][:, 0:width], rstd[:, t:t + 1], s_buf[:, t, 0:width],
                        ALU.mult, ALU.mult).then_inc(S("h_ready"), 1)

            def x_update(s, end_unit, factor):
                dve.wait_ge(S("tok0_done"), s + 1)
                for t in range(NT):
                    if t:
                        dve.wait_ge(S("unit_done"), end_unit)
                    for n in range(2):
                        xv = X[:, t, 512 * n:512 * n + 512]
                        STT(xv, B[D_BANK[t][n]][:], factor, xv, ALU.mult, ALU.add).then_inc(S("x_updated"), 1)

            def ffn(f):
                s, base = FFN_SUB[f], u_ffn[f]
                x_lo(XT[s], s)
                lo(base + 3)
                row_norm(s)
                for j in (4, 5, 6):
                    lo(base + j)
                up_product(f, 0, 512)
                lo(base + 7)
                with dve.Fori(0, 4) as turn:
                    lo(base + 8, turn)
                    lo(base + 9, turn)
                    hT_lo(HT[s], 0, 4, turn)
                    lo(base + 10, turn)
                    up_product(f, 1, 512, turn)
                    lo(base + 11, turn)
                lo(base + 24)
                hT_lo(HT[s] + 8, 16, 4)
                up_product(f, 5, 256)
                lo(base + 25)
                hT_lo(HT[s] + 10, 20, 2)
                for j in range(26, 36):
                    lo(base + j)
                x_update(s, base + 33, 0.5)

            nc.vector.memset(rs_a, 0.0).then_inc(S("hT_lo"), HT_FREE)
            for j in range(3):
                lo(j)
            dve.wait_ge(S("pos_loaded"), 16)
            nc.vector.tensor_copy(pos_rows[:, 1, :], pos_rows[:, 0, :].bitcast(i32)).then_inc(S("pos_float"), 1)
            dve.wait_ge(S("pos_sums"), 1)
            nc.vector.tensor_copy(pos_f, B[6][:, 0:NT]).then_inc(S("pos_ready"), 1)
            dve.wait_ge(S("params_ready"), 1)
            ffn(0)
            if stop_after == "ffn0":
                return

            b = u_ab
            dve.wait_ge(S("small_loaded"), 16 * N_SMALL)
            row_norm(1)
            dve.wait_ge(S("rstd_ready"), 2)
            for t in range(NT):
                TS(xs[:, t, :], X[:, t, :], rstd[:, t:t + 1], None, ALU.mult).then_inc(S("xs_ready"), 1)
            x_lo(XT[1], 1)
            lo(b + 3)
            dve.wait_ge(S("pm_out"), 2)
            LAT = Q_LORA + KV_LORA
            sq = tmp[:, 0:NT * LAT].rearrange("p (t n) -> p t n", n=LAT)
            link(TT(sq, PM[:, :, 0:LAT], PM[:, :, 0:LAT], ALU.mult))
            link(nc.vector.tensor_reduce(c_ss[:, 0:2], sq[:, :, 0:Q_LORA], AX.X, ALU.add))
            link(nc.vector.tensor_reduce(c_ss[:, 2:4], sq[:, :, Q_LORA:LAT], AX.X, ALU.add))
            link(rsqrt(c_rs[:, 0:2], c_ss[:, 0:2], 2, 1.0 / Q_LORA))
            link(rsqrt(c_rs[:, 2:4], c_ss[:, 2:4], 2, 1.0 / KV_LORA))
            for t in range(NT):
                for i, (c0, c1) in enumerate(((0, Q_LORA), (Q_LORA, LAT))):
                    TS(PM[:, t, c0:c1], PM[:, t, c0:c1], c_rs[:, 2 * i + t:2 * i + t + 1], None, ALU.mult
                       ).then_inc(S("c_normed"), 1)
            lo(b + 4)
            lo(b + 5)

            def conv(i):
                for s in range(2):
                    dve.wait_ge(S("tap_done"), 2 * i + 2)
                    src = B[2 + i % 2][:, 256 * s:256 * s + 256]
                    for back in (1, 2, 3):
                        y = yc[:, i % 2, s, back:SEQ]
                        w = convT[:, 2 * i + s, CONV - 1 - back:CONV - back]
                        ins = STT(y, src[:, 0:SEQ - back], w, y, ALU.mult, ALU.add)
                        if back < 3:
                            link(ins)
                    ins.then_inc(S("conv_done"), 1)

            conv(0)
            lo(b + 6)
            conv(1)
            for k in range(3):
                dve.wait_ge(S("cT_hi"), (2, 2, 3)[k])
                STT(hTl[:, k, :], (B[4][:, 256 * k:256 * k + 256] if k < 2 else B[5][:, 0:256]),
                    (qn_col[:, k:k + 1] if k < 2 else kvn_col), hTh[:, k, :].bitcast(f32),
                    ALU.mult, ALU.subtract).then_inc(S("cT_lo"), 1)
            lo(b + 7)
            lo(b + 8)
            lo(b + 9)
            for i in range(2, 6):
                conv(i)
                lo(b + 8 + i)
            lo(b + 14)
            lo(b + 15)

            fr = const("freq")
            link(TT(ang, bc(pos_f.unsqueeze(2), [P, NT, HALF]), bc(fr.unsqueeze(1), [P, NT, HALF]), ALU.mult))
            two_pi = 2 * np.pi
            p1 = float(np.float32(6.28125))
            p2 = float(np.float32(np.round((two_pi - p1) * 2 ** 21) / 2 ** 21))
            p3 = float(np.float32(two_pi - p1 - p2))
            link(TS(angk, ang, 1.0 / two_pi, 12582912.0, ALU.mult, ALU.add))
            link(TS(angk, angk, -12582912.0, None, ALU.add))
            for part in (p1, p2, p3):
                link(STT(ang, angk, -part, ang, ALU.mult, ALU.add))
            edge = float(np.nextafter(np.float32(np.pi), np.float32(0)))
            TS(ang, ang, edge, -edge, ALU.min, ALU.max).then_inc(S("angles"), 1)
            link(TT(sp, PM[:, :, AB_W + HEADS:AW], bc(dtb.unsqueeze(1), [P, NT, HEADS]), ALU.add))
            STT(egc, sp, -1.0, sp, ALU.mult, ALU.max).then_inc(S("a_abs"), 1)
            dve.wait_ge(S("sines"), 2)
            link(TT(cosT, cosT, cosT, ALU.mult))
            link(TS(cosT, cosT, -2.0, 1.0, ALU.mult, ALU.add))
            dve.wait_ge(S("gate_ln"), 1)
            link(STT(sp, sp, 0.0, gc, ALU.max, ALU.add))
            STT(gdec, sp, -1.0, bc(alog.unsqueeze(1), [P, NT, HEADS]), ALU.mult, ALU.mult
                ).then_inc(S("g_ready"), 1)
            link(TS(beta, beta, 1.0, None, ALU.add))
            link(nc.vector.reciprocal(beta, beta))

            M = NT * HEADS

            def norm_rope(buf, w_row, name):
                m = buf.rearrange("p t (h d) -> p (t h) d", d=QK)
                t3 = tmp.rearrange("p (m d) -> p m d", d=QK)
                link(TT(t3, m, m, ALU.mult))
                link(nc.vector.tensor_reduce(head_ss, t3, AX.X, ALU.add))
                link(rsqrt(head_ss, head_ss, M, 1.0 / QK))
                link(TT(m, m, bc(head_ss.unsqueeze(2), [P, M, QK]), ALU.mult))
                link(TT(m, m, bc(w_row.unsqueeze(1), [P, M, QK]), ALU.mult))
                v = [tmp[:, 256 * i:256 * i + 256].rearrange("p (t h d) -> p t h d", t=NT, h=HEADS) for i in range(4)]
                m4 = buf.rearrange("p t (h d) -> p t h d", d=QK)
                r1, r2 = m4[:, :, :, NOPE:NOPE + HALF], m4[:, :, :, NOPE + HALF:QK]
                for t in range(NT):
                    cb, sb_ = (bc(a[:, t:t + 1, :], [P, HEADS, HALF]) for a in (cosT, sinT))
                    for i, (r, a) in enumerate(((r1, cb), (r2, sb_), (r2, cb), (r1, sb_))):
                        link(TT(v[i][:, t], r[:, t], a, ALU.mult))
                link(TT(r1, v[0], v[1], ALU.subtract))
                TT(r2, v[2], v[3], ALU.add).then_inc(S(name), 1)

            dve.wait_ge(S("q_out"), 4)
            norm_rope(qm, qkn_q, "q_ready")
            dve.wait_ge(S("k_built"), 4)
            dve.wait_ge(S("q_ready"), 1)
            norm_rope(km, qkn_k, "k_ready")

            def head_norm(a, extra):
                a3 = a.rearrange("p t (h d) -> p (t h) d", d=DK)
                t3 = yc.rearrange("p a b n -> p (a b n)").rearrange("p (m d) -> p m d", d=DK)
                link(TT(t3, a3, a3, ALU.mult))
                link(nc.vector.tensor_reduce(head_ss, t3, AX.X, ALU.add))
                link(rsqrt(head_ss, head_ss, M, 1.0, extra))
                return TT(a3, a3, bc(head_ss.unsqueeze(2), [P, M, DK]), ALU.mult)

            def per_head(out_, a, w):
                return TT(out_.rearrange("p t (h d) -> p (t h) d", d=DK), a.rearrange("p t (h d) -> p (t h) d", d=DK),
                          bc(w.rearrange("p t h -> p (t h)").unsqueeze(2), [P, M, DK]), ALU.mult)

            future = const("future")
            for h in range(HEADS):
                src = B[6 + h % 2][:, 0:384].rearrange("p (b n) -> p b n", n=P)
                dve.wait_ge(S("score_sums"), h + 1)
                if h:
                    dve.wait_ge(S("exp_done"), 2 * h)
                TT(scores[:, 0:2, :], src[:, 0:2, :], bc(future.unsqueeze(1), [P, 2, P]), ALU.add
                   ).then_inc(S("score_out"), 1)
                nc.vector.tensor_copy(scores[:, 2, :], src[:, 2, :]).then_inc(S("score_out"), 1)
                dve.wait_ge(S("score_out"), 2 * h + 2)
                link(nc.vector.tensor_reduce(smax, scores, AX.X, ALU.max))
                link(TT(smax[:, 1:2], smax[:, 1:2], smax[:, 2:3], ALU.max))
                TS(nbias, smax[:, 0:2], -(float(QK) ** -0.5), None, ALU.mult).then_inc(S("softmax_in"), 1)
            dve.wait_ge(S("nt_out"), 6)
            link(head_norm(QKVn[0], float(DK) ** -0.5))
            link(head_norm(QKVn[1], 1.0))
            link(per_head(QKVn[2], QKVn[2], beta))
            dve.wait_ge(S("exp_done"), 2 * HEADS)
            link(nc.vector.reciprocal(rden, row_sum))
            dve.wait_ge(S("pv_sums"), HEADS)
            for t in range(NT):
                TT(Y[:, t, 0:512].rearrange("p (h d) -> p h d", d=VDIM),
                   B[t][:].rearrange("p (h d) -> p h d", d=VDIM),
                   bc(rden[:, t, :].unsqueeze(2), [P, HEADS, VDIM]), ALU.mult).then_inc(S("y_mla"), 1)

            gf = gdec.rearrange("p t h -> p (t h)")
            TT(gU.rearrange("p (m j) -> p m j", j=64), bc(gf.unsqueeze(2), [P, M, 64]),
               bc(cumul.unsqueeze(1), [P, M, 64]), ALU.mult).then_inc(S("gu_ready"), 1)
            dve.wait_ge(S("gc_sums"), 2)
            gcf, ekf = (a.rearrange("p t h -> p (t h)") for a in (gc, ek))
            for c in range(2):
                r = slice(64 * c, 64 * c + 64)
                link(nc.vector.tensor_copy(gcf[r, :], B[2 + c][r, 0:16]))
                link(TT(ekf[r, :], B[2 + c][r, 16:32], gcf[r, :], ALU.subtract))
            link(TS(ekf, ekf, 0.0, None, ALU.add))
            nc.vector.tensor_copy(rs_a, gcf).then_inc(S("gc_ready"), 1)
            D3 = Dec.rearrange("p (m j) -> p m j", j=64)
            for t in range(NT):
                for c in range(2):
                    r = slice(64 * c, 64 * c + 64)
                    dve.wait_ge(S("gr_sums"), 2 * t + c + 1)
                    link(TT(D3[r, 8 * t:8 * t + 8, :], B[4 + 2 * t + c][r, :].rearrange("p (h j) -> p h j", j=64),
                            bc(gcf[r, 8 * t:8 * t + 8].unsqueeze(2), [64, 8, 64]), ALU.subtract))
            TS(Dec, Dec, 0.0, None, ALU.max).then_inc(S("dec_diff"), 1)
            dve.wait_ge(S("decay_exps"), 2)
            link(TT(begc, beta, egc, ALU.mult))
            per_head(qd, QKVn[0], egc).then_inc(S("gdn_in"), 1)
            per_head(kbe.rearrange("p (t n) -> p t n", t=NT), QKVn[1], begc).then_inc(S("gdn_in"), 1)
            per_head(kt.rearrange("p (t n) -> p t n", t=NT), QKVn[1], ek).then_inc(S("gdn_in"), 1)
            dve.wait_ge(S("dec_exp"), 1)
            link(TT(D3, D3, bc(const("causal").unsqueeze(1), [P, M, 64]), ALU.mult))
            link(TT(DecB.rearrange("p (m j) -> p m j", j=64), D3,
                    bc(beta.rearrange("p t h -> p (t h)").unsqueeze(2), [P, M, 64]), ALU.mult))
            for n, (dst, decay) in enumerate(((Lm, DecB), (Am, Dec))):
                for odd in range(2):
                    dve.wait_ge(S("gram_sums"), 2 * n + odd + 1)
                    view = [a.rearrange("p (q o j) -> p q o j", o=2, j=64)[:, :, odd, :] for a in (dst, decay)]
                    TT(view[0], B[4 + 2 * n + odd][:].rearrange("p (q j) -> p q j", j=64), view[1], ALU.mult
                       ).then_inc(S("la_ready"), 1)
            dve.wait_ge(S("la_ready"), 4)
            m3 = lambda a: a.rearrange("p (m j) -> p m j", j=64)
            eye = bc(const("eye64").unsqueeze(1), [P, M, 64])
            link(TT(m3(Dm), m3(Lm), bc(const("first").unsqueeze(1), [P, M, 64]), ALU.mult))
            TT(m3(Dm), eye, m3(Dm), ALU.subtract).then_inc(S("d_ready"), 1)
            dve.wait_ge(S("lt_ready"), 4)
            link(TT(m3(DT), m3(LT), bc(const("level1").unsqueeze(1), [P, M, 64]), ALU.mult))
            TT(m3(DT), eye, m3(DT), ALU.subtract).then_inc(S("d_ready"), 1)
            for n in range(5):
                m, o = 4 * (n % 2), 4 * ((n + 1) % 2)
                for t in range(NT):
                    for i, dst in enumerate((Dm, DT)):
                        if n == 4 and i == 0:
                            continue
                        for c in range(2):
                            r = slice(64 * c, 64 * c + 64)
                            bank = (o if t == 0 else m) + 2 * i + c
                            dve.wait_ge(S("y_sums") if i == 0 else S("yt_sums"), 4 * n + 2 * t + c + 1)
                            v = dst[r, 512 * t:512 * t + 512]
                            TT(v, v, B[bank][r, :], ALU.subtract).then_inc(
                                S("d_merged") if i == 0 else S("dt_merged"), 1)
            link(nc.vector.memset(state, 0.0))
            nc.vector.memset(v_new, 0.0).then_inc(S("state_zero"), 1)
            for n in range(3):
                for odd in range(2):
                    r, e = slice(64 * odd, 64 * odd + 64), slice(64 * odd, 64 * odd + 64)
                    decay = bc(eg[r, n, :].unsqueeze(2), [64, PAIRS, 64])
                    TT(s_dec[r, :, e], state[r, :, e], decay, ALU.mult).then_inc(S("state_decayed"), 1)
                dve.wait_ge(S("s_sums"), n + 1)
                dve.wait_ge(S("state_decayed"), 2 * n + 2)
                for odd in range(2):
                    r, e = slice(64 * odd, 64 * odd + 64), slice(64 * odd, 64 * odd + 64)
                    TT(state[r, :, e], s_dec[r, :, e],
                       B[2][r, :].rearrange("p (q e) -> p q e", e=P)[:, :, e], ALU.add
                       ).then_inc(S("state_ready"), 1)
                dve.wait_ge(S("state_ready"), 2 * n + 2)
            dve.wait_ge(S("o_out"), 4)
            O4 = Y[:, :, 512:1024].rearrange("p t (h d) -> p t h d", d=DK)
            d4 = Dec.rearrange("p (t h d) -> p t h d", t=NT, d=DK)
            link(TT(d4, O4, O4, ALU.mult))
            link(nc.vector.tensor_reduce(head_ss, m3(Dec), AX.X, ALU.add))
            link(rsqrt(head_ss, head_ss, M, 1.0 / DK))
            hs = head_ss.rearrange("p (t h) -> p t h", t=NT).unsqueeze(3)
            link(TT(O4, O4, bc(hs, [P, NT, HEADS, DK]), ALU.mult))
            dve.wait_ge(S("z_weighted"), 1)
            TT(Y[:, :, 512:1024], Y[:, :, 512:1024], SZ, ALU.mult).then_inc(S("y_gdn"), 1)
            x_lo(2)
            for j in range(16, 19):
                lo(b + j)
            x_update(1, b + 16, 1.0)
            if stop_after == "ab":
                return

            ffn(1)
            ffn(2)

            b = u_sg
            x_lo(XT[4], 4)
            lo(b + 3)
            row_norm(4)
            for c in range(4):
                lo(b + 2 * c + 4)
                dve.wait_ge(S("v_squared"), 4 * c + 4)
                link(rsqrt(v_ss, v_ss, 4, 1.0 / CG))
                v4 = V[:, :, 512 * c:512 * c + 512].rearrange("p t (g n) -> p t g n", n=CG)
                r4 = v_ss.rearrange("p (t g) -> p t g", g=2).unsqueeze(3)
                TT(v4, v4, bc(r4, [P, NT, 2, CG]), ALU.mult).then_inc(S("v_scaled"), 1)
                lo(b + 2 * c + 5)
            for c in range(4):
                lo(b + 8 + 2 * c + 4)
                if c >= 1:
                    hT_lo(HT[4] + 2 * (c - 1), 4 * (c - 1), 4)
                dve.wait_ge(S("u_gelu"), 2 * c + 2)
                dve.wait_ge(S("gate_ready"), 4 * c + 4)
                TT(h_buf, s_buf, V[:, :, 512 * c:512 * c + 512], ALU.mult).then_inc(S("y_ready"), 1)
                lo(b + 8 + 2 * c + 5)
            hT_lo(HT[4] + 6, 12, 4)
            for j in range(20, 27):
                lo(b + j)
            x_update(4, b + 24, 1.0)
            ffn(3)

        @block.tensor
        def _(pe):
            mm, transpose = nc.tensor.matmul, nc.tensor.transpose

            def split_mm(out_ap, lh, ll, rh, rl, first, last):
                mm(out_ap, lh, rh, start=first, stop=False)
                mm(out_ap, lh, rl, start=False, stop=False)
                return mm(out_ap, ll, rh, start=False, stop=last)

            def slot(j):
                kt, width, _ = units[j]
                return unit_view(whi, j, kt, width), unit_view(wlo, j, kt, width)

            def begin(j, turn=0):
                pe.wait_ge(S("lo_ready"), turn * SLOTS + (j + 1))

            def gemm(j, banks, k0, k_all, srcs, turn=0):
                kt, width, _ = units[j]
                wh, wl = slot(j)
                sh, sl = srcs
                begin(j, turn)
                for k in range(kt):
                    for t in range(NT):
                        tok = slice(P * t, P * t + P)
                        last = split_mm(B[banks[t]][:, 0:width], sh[:, k0 + k, tok], sl[:, k0 + k, tok],
                                        wh[:, k, :], wl[:, k, :], k0 + k == 0, k0 + k == k_all - 1)
                last.then_inc(S("unit_done"), 1)

            def down(base, n_units, srcs, done_before=0, upto=None):
                sh, sl = srcs
                for i in range(done_before, n_units if upto is None else upto):
                    j = base + i
                    wh, wl = slot(j)
                    begin(j)
                    final = i == n_units - 1
                    order = [(k, t) for t in range(NT) for k in range(2)] if final else \
                            [(k, t) for k in range(2) for t in range(NT)]
                    for k, t in order:
                        kk, tok = 2 * i + k, slice(P * t, P * t + P)
                        a, z = kk == 0, kk == 2 * n_units - 1
                        outs = [B[D_BANK[t][n]][:] for n in range(2)]
                        cols = [slice(0, 512), slice(512, 1024)]
                        for n in range(2):
                            mm(outs[n], sh[:, kk, tok], wh[:, k, cols[n]], start=a, stop=False)
                            mm(outs[n], sh[:, kk, tok], wl[:, k, cols[n]], start=False, stop=False)
                        for n in range(2):
                            last = mm(outs[n], sl[:, kk, tok], wh[:, k, cols[n]], start=False, stop=z)
                        if final and z and t == 0:
                            last.then_inc(S("tok0_done"), 1)
                    last.then_inc(S("unit_done"), 1)

            def x_transposes(xi, src, waits):
                for t in range(NT):
                    waits(t)
                    for k in range(KD):
                        last = transpose(B[X_BANK[k // 2]][:, 256 * (k % 2) + P * t:256 * (k % 2) + P * t + P],
                                         src[:, t, P * k:P * k + P], ident)
                        if t == NT - 1 and k % 2:
                            last.then_inc(S("xT_sums"), 1)

            def h_transposes(n_blocks, banks_read, turn=0):
                for bank in range(n_blocks // 2):
                    pe.wait_ge(S("hT_lo"), turn * 2 + (HT_FREE + banks_read + bank + 1))
                    for i in range(2):
                        for t in range(NT):
                            f = P * (2 * bank + i)
                            last = transpose(B[4 + bank][:, 256 * i + P * t:256 * i + P * t + P],
                                             h_buf[:, t, f:f + P], ident)
                    last.then_inc(S("hT_sums"), 1)

            XS, HS = (xTh, xTl), (hTh, hTl)

            def ffn(f):
                s, base = FFN_SUB[f], u_ffn[f]
                if s == 0:
                    def waits(t):
                        if t == 0:
                            pe.wait_ge(S("x_loaded"), 16)
                else:
                    def waits(t):
                        pe.wait_ge(S("x_updated"), 4 * (s - 1) + 2 * (t + 1))
                x_transposes(XT[s], X, waits)
                for i, banks in ((0, (0, 1)), (2, (2, 3))):
                    for u in range(2):
                        pe.wait_ge(S("xT_lo"), 8 * XT[s] + (4 * u + 4 if i == 0 else 8))
                        gemm(base + i + u, banks, 4 * u, KD, XS)
                with pe.Fori(0, 4) as turn:
                    pe.wait_ge(S("silu_done"), turn * 2 + (12 * f + 2))
                    gemm(base + 4, (0, 1), 0, KD, XS, turn)
                    gemm(base + 5, (0, 1), 4, KD, XS, turn)
                    pe.wait_ge(S("h_ready"), turn * 2 + (12 * f + 2))
                    h_transposes(4, HT[s] - 2, turn)
                    gemm(base + 6, (2, 3), 0, KD, XS, turn)
                    gemm(base + 7, (2, 3), 4, KD, XS, turn)
                pe.wait_ge(S("silu_done"), 12 * f + 10)
                gemm(base + 20, (0, 1), 0, KD, XS)
                pe.wait_ge(S("h_ready"), 12 * f + 10)
                h_transposes(4, HT[s] + 6)
                gemm(base + 21, (2, 3), 0, KD, XS)
                pe.wait_ge(S("silu_done"), 12 * f + 12)
                pe.wait_ge(S("hT_lo"), HT_FREE + HT[s] + 10)
                down(base + 22, 11, HS, upto=2)
                pe.wait_ge(S("h_ready"), 12 * f + 12)
                h_transposes(2, HT[s] + 8)
                down(base + 22, 11, HS, done_before=2, upto=10)
                pe.wait_ge(S("hT_lo"), HT_FREE + HT[s] + 11)
                down(base + 22, 11, HS, done_before=10)


            pe.wait_ge(S("const_loaded"), 16)
            pe.wait_ge(S("rows_loaded"), 80)
            transpose(B[7][:, 0:N_ROWS], param_rows[:], ident[0:N_ROWS, 0:N_ROWS]).then_inc(S("param_sums"), 1)
            pe.wait_ge(S("pos_float"), 1)
            transpose(B[6][:, 0:NT], pos_rows[:, 1, :], ident[0:NT, 0:NT]).then_inc(S("pos_sums"), 1)
            ffn(0)
            if stop_after == "ffn0":
                return

            b = u_ab
            x_transposes(XT[1], xs, lambda t: pe.wait_ge(S("xs_ready"), t + 1))
            for u in range(2):
                pe.wait_ge(S("xT_lo"), 8 * XT[1] + 4 * u + 4)
                gemm(b + u, (0, 1), 4 * u, KD, XS)

            def channels(i):
                j = C_UNIT[i]
                wh, wl = slot(j)
                begin(j)
                if i >= 2:
                    pe.wait_ge(S("conv_done"), 2 * (i - 1))
                for s in range(2):
                    cols = slice(P * s, P * s + P)
                    for k in range(KD):
                        last = split_mm(B[2 + i % 2][:, 256 * s:256 * s + 256], wh[:, k, cols], wl[:, k, cols],
                                        xTh[:, k, :], xTl[:, k, :], k == 0, k == KD - 1)
                last.then_inc(S("unit_done"), 1)

            def to_tokens(i):
                pe.wait_ge(S("yc_ready"), i + 1)
                if i == 0:
                    pe.wait_ge(S("kv_out"), 2)
                else:
                    pe.wait_ge(S("nt_out"), i)
                for s in range(2):
                    for t in range(NT):
                        last = transpose(B[5][:, 256 * t + P * s:256 * t + P * s + P],
                                         yc[:, i % 2, s, P * t:P * t + P], ident)
                last.then_inc(S("nt_sums"), 1)

            channels(0)
            channels(1)
            pe.wait_ge(S("c_normed"), 4)
            for k in range(3):
                for t in range(NT):
                    dst = B[4][:, 256 * k + P * t:256 * k + P * t + P] if k < 2 else B[5][:, P * t:P * t + P]
                    last = transpose(dst, PM[:, t, P * k:P * k + P], ident)
                if k:
                    last.then_inc(S("cT_sums"), 1)
            pe.wait_ge(S("cT_lo"), 3)
            begin(b + 4)
            wh, wl = slot(b + 4)
            for t in range(NT):
                if t:
                    pe.wait_ge(S("pm_out"), 2)
                for n, (c0, c1) in enumerate(((0, 512), (512, 768))):
                    for k in range(2):
                        tok = slice(P * t, P * t + P)
                        last = split_mm(B[(6, 0)[t] + n][:, 0:c1 - c0], hTh[:, k, tok], hTl[:, k, tok],
                                        wh[:, k, c0:c1], wl[:, k, c0:c1], k == 0, k == 1)
            last.then_inc(S("unit_done"), 1)
            begin(b + 5)
            wh, wl = slot(b + 5)
            for t in range(NT):
                if t:
                    pe.wait_ge(S("q_out"), 2)
                for n in range(2):
                    tok, c0 = slice(P * t, P * t + P), 512 * n
                    last = split_mm(B[(4, 6)[t] + n][:], hTh[:, 2, tok], hTl[:, 2, tok],
                                    wh[:, 0, c0:c0 + 512], wl[:, 0, c0:c0 + 512], True, True)
                if t == 0:
                    last.then_inc(S("kv_sums"), 1)
            last.then_inc(S("unit_done"), 1)
            channels(2)
            to_tokens(0)
            channels(3)
            to_tokens(1)
            channels(4)
            to_tokens(2)
            channels(5)
            to_tokens(3)
            pe.wait_ge(S("q_out"), 4)
            for u in range(2):
                gemm(b + 10 + u, (0, 1), 4 * u, KD, XS)
            to_tokens(4)
            to_tokens(5)

            for i in range(8):
                src, t, g = (qm, km)[i // 4], i // 2 % 2, i % 2
                pe.wait_ge(S("q_ready") if i < 4 else S("k_ready"), 1)
                if i == 0:
                    pe.wait_ge(S("kv_out"), 4)
                if i >= 2:
                    pe.wait_ge(S("qkT_out"), i - 1)
                for h in range(4):
                    last = transpose(B[(4, 6)[i % 2]][0:QK, P * h:P * h + P],
                                     src[:, t, QK * (4 * g + h):QK * (4 * g + h) + QK], ident)
                last.then_inc(S("qkT_sums"), 1)

            def head_scores(h):
                if h < 2:
                    pe.wait_ge(S("qkT_out"), 8)
                else:
                    pe.wait_ge(S("score_out"), 2 * (h - 1))
                for i, (tq, tk) in enumerate(((0, 0), (1, 1), (1, 0))):
                    last = mm(B[6 + h % 2][:, P * i:P * i + P], qTm[0:QK, h, P * tq:P * tq + P],
                              kTm[0:QK, h, P * tk:P * tk + P], start=True, stop=True)
                last.then_inc(S("score_sums"), 1)

            head_scores(0)
            head_scores(1)
            kv_v = kvm.rearrange("p t (h d) -> p t h d", d=NOPE + VDIM)[:, :, :, NOPE:]
            for h in range(HEADS):
                pe.wait_ge(S("exp_done"), 2 * h + 2)
                if h:
                    pe.wait_ge(S("pT_out"), h)
                for i in range(3):
                    last = transpose(B[4][:, P * i:P * i + P], probs[:, i, :], ident)
                last.then_inc(S("pT_sums"), 1)
                if h + 2 < HEADS:
                    head_scores(h + 2)
                pe.wait_ge(S("pT_out"), h + 1)
                if h == 0:
                    pe.wait_ge(S("z_out"), 2)
                e = slice(VDIM * h, VDIM * h + VDIM)
                for t, i, tk, a, z in ((0, 0, 0, True, True), (1, 1, 1, True, False), (1, 2, 0, False, True)):
                    last = mm(B[t][:, e], pT[:, h % 2, P * i:P * i + P], kv_v[:, tk, h, :], start=a, stop=z)
                last.then_inc(S("pv_sums"), 1)

            HC = [slice(0, 64), slice(64, 128)]
            pe.wait_ge(S("g_ready"), 1)
            for c in range(2):
                r = HC[c]
                g2 = gdec.rearrange("p t h -> p (t h)")
                mm(B[2 + c][r, 0:16], cumul[r, :], g2[r, :], start=True, stop=True)
                mm(B[2 + c][r, 16:32], ones64[r, :], g2[r, :], start=True, stop=True)
                for r2 in HC:
                    last = mm(B[2 + c][r2, 32:48], ones64[r, :], g2[r, :], start=True, stop=True)
                last.then_inc(S("gc_sums"), 1)
            pe.wait_ge(S("gu_ready"), 1)
            for t in range(NT):
                for c in range(2):
                    if t == 0 and c == 0:
                        pe.wait_ge(S("softmax_in"), HEADS)
                    mm(B[4 + 2 * t + c][HC[c], :], ones64[HC[c], :], gU[HC[c], 512 * t:512 * t + 512],
                       start=True, stop=True).then_inc(S("gr_sums"), 1)
            pe.wait_ge(S("y_mla"), 2)
            for i, src in enumerate((QKVn[0], QKVn[1], qd)):
                if i == 2:
                    pe.wait_ge(S("gdn_in"), 1)
                for g in range(2):
                    n = 2 * i + g
                    if n >= 2:
                        pe.wait_ge(S("dT_out"), n - 1)
                    for q in range(2):
                        for t in range(NT):
                            last = transpose(B[n % 2][:, 256 * q + P * t:256 * q + P * t + P],
                                             src[:, t, P * (2 * g + q):P * (2 * g + q) + P], ident)
                    last.then_inc(S("dT_sums"), 1)
            pe.wait_ge(S("dT_out"), 4)
            pe.wait_ge(S("dec_diff"), 1)
            for n, left in enumerate((kT, qT)):
                for odd in range(2):
                    r = HC[odd]
                    for t in range(NT):
                        for q in range(PAIRS):
                            for c in range(2):
                                tok = slice(P * t + 64 * c, P * t + 64 * c + 64)
                                col = 64 * (PAIRS * t + q)
                                last = mm(B[4 + 2 * n + odd][HC[c], col:col + 64], left[r, q, tok],
                                          kT[r, q, tok], start=True, stop=True)
                    last.then_inc(S("gram_sums"), 1)
            pe.wait_ge(S("dT_out"), 6)
            eye = const("eye64")

            def problems(t, bank, lhs, rhs, name):
                for h in range(HEADS):
                    m = slice(64 * (8 * t + h), 64 * (8 * t + h) + 64)
                    for c in range(2):
                        last = mm(B[bank + c][HC[c], 64 * h:64 * h + 64], lhs[HC[c], m],
                                  (eye[HC[c], :] if rhs is None else rhs[HC[c], m]), start=True, stop=True)
                        if h == HEADS - 1:
                            last.then_inc(S(name), 1)

            pe.wait_ge(S("la_ready"), 4)
            pe.wait_ge(S("eg_ready"), 4)
            pe.wait_ge(S("gc_ready"), 1)
            for n, src in enumerate((Lm, Am)):
                for t in range(NT):
                    problems(t, 4 * n + 2 * t, src, None, "la_sums")
            for n in range(5):
                lof = Loff[n % 2]
                m, o = 4 * (n % 2), 4 * ((n + 1) % 2)
                pe.wait_ge(S("loff_ready"), n + 1)
                if n == 0:
                    pe.wait_ge(S("d_ready"), 2)
                    pe.wait_ge(S("at_ready"), 4)
                for t in range(NT):
                    if n:
                        pe.wait_ge(S("d_merged"), 4 * n - 2 + 2 * t)
                        if t == 1:
                            pe.wait_ge(S("dt_merged"), 4 * n - 2)
                    problems(t, m + 2 * t, lof, Dm, "m1_sums")
                for t in range(NT):
                    pe.wait_ge(S("m1_ready"), 4 * n + 2 * t + 2)
                    if n:
                        pe.wait_ge(S("dt_merged"), 4 * n - 2 + 2 * t)
                    first = o if t == 0 else m
                    if t == 1:
                        pe.wait_ge(S("m1_ready"), 4 * n + 4)
                    if n < 4:
                        problems(t, first, DT, M1, "y_sums")
                    if n and t == 0:
                        pe.wait_ge(S("dt_merged"), 4 * n)
                    problems(t, first + 2, M1, DT, "yt_sums")
            pe.wait_ge(S("dt_merged"), 20)
            for c in range(2):
                for t in range(NT):
                    for h in range(HEADS):
                        m = slice(64 * (8 * t + h), 64 * (8 * t + h) + 64)
                        col = 64 * (PAIRS * t + h // 2)
                        last = mm(B[4 + c][HC[h % 2], col:col + 64], kbe[HC[c], 512 * t + 64 * h:512 * t + 64 * h + 64],
                                  DT[HC[c], m], start=True, stop=True)
                last.then_inc(S("w_sums"), 1)
            pe.wait_ge(S("w_ready"), 2)
            pe.wait_ge(S("state_zero"), 1)
            for n in range(4):
                t, c = n // 2, n % 2
                r, tok = HC[c], slice(P * t + 64 * c, P * t + 64 * c + 64)
                if n:
                    pe.wait_ge(S("v_new_ready"), n)
                for h in range(HEADS):
                    last = mm(B[0][r, 64 * h:64 * h + 64], DT[r, 64 * (8 * t + h):64 * (8 * t + h) + 64],
                       QKVn[2][r, t, 64 * h:64 * h + 64], start=h == 0, stop=n == 0, skip_group_check=True)
                if n:
                    pe.wait_ge(S("state_ready"), 2 * n)
                    pe.wait_ge(S("o_out"), n)
                    for q in range(PAIRS):
                        last = mm(B[0][r, P * q:P * q + P], wT[:, q, tok], state[:, q, :], start=False, stop=True,
                                  skip_group_check=True)
                last.then_inc(S("v_sums"), 1)
                for q in range(PAIRS):
                    if n:
                        mm(B[1][r, P * q:P * q + P], qdT[:, q, tok], state[:, q, :], start=q == 0, stop=False,
                           skip_group_check=True)
                pe.wait_ge(S("v_new_ready"), n + 1)
                for h in range(HEADS):
                    last = mm(B[1][r, 64 * h:64 * h + 64], AT[r, 64 * (8 * t + h):64 * (8 * t + h) + 64],
                              v_new[r, 64 * h:64 * h + 64], start=(n == 0 and h == 0), stop=True,
                              skip_group_check=True)
                last.then_inc(S("o_sums"), 1)
                if n < 3:
                    for q in range(PAIRS):
                        last = mm(B[2][:, P * q:P * q + P], kt[r, 512 * t + P * q:512 * t + P * q + P],
                                  v_new[r, P * q:P * q + P], start=True, stop=True)
                    last.then_inc(S("s_sums"), 1)
            x_transposes(2, Y, lambda t: pe.wait_ge(S("y_gdn"), 1))
            pe.wait_ge(S("xT_lo"), 24)
            down(b + 12, 4, XS)
            if stop_after == "ab":
                return

            ffn(1)
            ffn(2)

            b = u_sg
            x_transposes(XT[4], X, lambda t: pe.wait_ge(S("x_updated"), 12 + 2 * (t + 1)))

            def gates(c):
                pe.wait_ge(S("v_ready"), c + 1)
                if c:
                    pe.wait_ge(S("gate_ready"), 4 * c)
                else:
                    pe.wait_ge(S("wsT_ready"), 2)
                for t in range(NT):
                    for g in (2 * c, 2 * c + 1):
                        last = mm(B[6 + t][:, CG * (g % 2):CG * (g % 2) + CG], wsT[:, g, :],
                                  V[:, t, CG * g:CG * g + CG], start=True, stop=True)
                    last.then_inc(S("gate_sums"), 1)

            for c in range(8):
                for u in range(2):
                    if c == 0:
                        pe.wait_ge(S("xT_lo"), 8 * XT[4] + 4 * u + 4)
                    if c >= 2 and u == 0:
                        pe.wait_ge(S("v_gelu"), min(2 * (c - 1), 8))
                        if c >= 6:
                            pe.wait_ge(S("u_gelu"), 2 * (c - 5))
                    gemm(b + 2 * c + u, (2 * (c % 2), 2 * (c % 2) + 1), 4 * u, KD, XS)
                if c == 0:
                    pe.wait_ge(S("ws_masked"), 1)
                    for g in range(GROUPS):
                        last = transpose(B[6 + g // 4][:, P * (g % 4):P * (g % 4) + P], ws_raw[:, g, :], ident)
                        if g % 4 == 3:
                            last.then_inc(S("wsT_sums"), 1)
                elif c <= 4:
                    gates(c - 1)
                else:
                    pe.wait_ge(S("y_ready"), c - 4)
                    h_transposes(4, HT[4] + 2 * (c - 5) - 2)
            pe.wait_ge(S("gate_ready"), 16)
            pe.wait_ge(S("u_gelu"), 8)
            pe.wait_ge(S("hT_lo"), HT_FREE + HT[4] + 6)
            down(b + 16, 8, HS, upto=2)
            pe.wait_ge(S("y_ready"), 4)
            h_transposes(4, HT[4] + 4)
            down(b + 16, 8, HS, done_before=2, upto=6)
            pe.wait_ge(S("hT_lo"), HT_FREE + HT[4] + 8)
            down(b + 16, 8, HS, done_before=6)
            ffn(3)


_INS = ["x", "positions", "norm_w", "ffn_w_gate", "ffn_w_up", "ffn_w_down", "ab_w_in", "mla_q_norm",
        "mla_w_q_b", "mla_kv_norm", "mla_w_kv_b", "mla_qk_norm_q", "mla_qk_norm_k", "gdn_conv_w",
        "gdn_a_log", "gdn_dt_bias", "gdn_out_norm", "ab_w_out", "sg_w_in", "sg_v_norm", "sg_w_s",
        "sg_b_s", "sg_w_out"]


def kernel(**inputs):
    import concourse.bacc as bacc
    from concourse.bass_utils import run_bass_kernel_spmd

    nc = bacc.Bacc("TRN2", target_bir_lowering=False, num_devices=1)
    arrays, args = {}, []
    for name, a in [(n, inputs[n]) for n in _INS] + [("constants", constants()[0])]:
        a = np.ascontiguousarray(a)
        arrays[f"in_{name}"] = a
        args.append(nc.dram_tensor(f"in_{name}", a.shape, mybir.dt.from_np(a.dtype), kind="ExternalInput").ap())
    args.append(nc.dram_tensor("out_x", (1, SEQ, D_MODEL), mybir.dt.float32, kind="ExternalOutput").ap())
    build_trunk(nc, *args)
    r = run_bass_kernel_spmd(nc, [arrays], core_ids=[0])
    return r.results[0]["out_x"]
```

```python
import numpy as np
import concourse.bass as bass
from concourse import mybir
from contextlib import ExitStack

P = 128
D_MODEL, SEQ, D_FF = 1024, 256, 2816
NT = SEQ // P
KD = D_MODEL // P
KF = D_FF // P
Q_LORA, KV_LORA, NOPE, ROPE, VDIM = 256, 128, 64, 32, 64
QK = NOPE + ROPE
HALF = ROPE // 2
HEADS = 8
DK = 64
CHUNK = 64
CONV = 4
PAIRS = HEADS // 2
AB_W = Q_LORA + KV_LORA + ROPE
QKV0 = AB_W
Z0 = QKV0 + 3 * HEADS * DK
BA0 = Z0 + HEADS * DK
AW = AB_W + 2 * HEADS
SGW, GROUPS, CG = 2048, 8, 256
EPS = 1e-6
SLOT = 2048
SLOTS = 4
LEVELS = (1, 2, 4, 8, 16, 32)


def constants():
    p = np.arange(P)[:, None]
    i64, i128 = np.arange(64)[None, :], np.arange(P)[None, :]
    q = p % 64
    parts = [
        ("ident", i128 == p),
        ("cumul", q <= i64),
        ("ones", np.ones((P, 64))),
        ("causal", i64 <= q),
        ("eye64", i64 == q),
        ("first", (q // 2 == i64 // 2) & (q % 2 == 1) & (i64 % 2 == 0)),
    ]
    for b in LEVELS:
        up = (q // (2 * b) == i64 // (2 * b)) & ((i64 // b) % 2 == 1) & ((q // b) % 2 == 0)
        parts.append((f"level{b}", up))
    parts.append(("future", np.where(i128 <= p, 0.0, -1.0e30)))
    parts.append(("tril128", i128 <= p))
    freq = np.float32(10000.0) ** (-np.arange(0, ROPE, 2, dtype=np.float32) / np.float32(ROPE))
    parts.append(("freq", np.broadcast_to(freq, (P, HALF))))
    at, where = 0, {}
    for name, a in parts:
        where[name] = (at, a.shape[1])
        at += a.shape[1]
    return np.ascontiguousarray(np.concatenate([a.astype(np.float32) for _, a in parts], axis=1)), where


def build_trunk(nc, x, positions, norm_w, w_gate, w_up, w_down, ab_in, q_norm, w_q_b, kv_norm, w_kv_b,
                qk_norm_q, qk_norm_k, conv_w, a_log, dt_bias, gdn_norm, ab_out, sg_in, sg_norm, sg_ws,
                sg_bs, sg_out, const_dram, out, stop_after=None):
    f32, f32r, i32 = mybir.dt.float32, mybir.dt.float32r, mybir.dt.int32
    ALU, ACT, AX = mybir.AluOpType, mybir.ActivationFunctionType, mybir.AxisListType
    const_at = constants()[1]
    n_const = const_dram.shape[1]
    ds = bass.ds

    def rows(w, k0, kt, c0, cw):
        return w[k0 * P:(k0 + kt) * P, :].rearrange("(k p) n -> p k n", p=P)[:, :, c0:c0 + cw]

    units = []

    def unit(kt, width, *pieces):
        units.append((kt, width, pieces))
        return len(units) - 1

    def ffn_units(l, s):
        g, u, d = w_gate[l, s], w_up[l, s], w_down[l, s]
        base = len(units)
        for c in range(5):
            for w in (g, u):
                for k0 in (0, 4):
                    unit(4, 512, (0, rows(w, k0, 4, 512 * c, 512)))
        for w in (g, u):
            unit(8, 256, (0, rows(w, 0, 8, 2560, 256)))
        for k in range(KF // 2):
            unit(2, 1024, (0, rows(d, 2 * k, 2, 0, 1024)))
        return base

    def ab_units():
        w = ab_in[0]
        base = len(units)
        for k0 in (0, 4):
            unit(4, AW, (0, rows(w, k0, 4, 0, AB_W)), (AB_W, rows(w, k0, 4, BA0, 2 * HEADS)))
        for c in (0, 1, 2):
            unit(8, 256, (0, rows(w, 0, 8, QKV0 + 256 * c, 256)))
        unit(2, 768, (0, rows(w_q_b[0], 0, 2, 0, 768)))
        unit(1, 1024, (0, rows(w_kv_b[0], 0, 1, 0, 1024)))
        for c in range(3, 6):
            unit(8, 256, (0, rows(w, 0, 8, QKV0 + 256 * c, 256)))
        for k0 in (0, 4):
            unit(4, 512, (0, rows(w, k0, 4, Z0, 512)))
        for k in range(4):
            unit(2, 1024, (0, rows(ab_out[0], 2 * k, 2, 0, 1024)))
        return base

    def sg_units():
        base = len(units)
        for c in (4, 5, 6, 7, 0, 1, 2, 3):
            for k0 in (0, 4):
                unit(4, 512, (0, rows(sg_in[0], k0, 4, 512 * c, 512)))
        for k in range(8):
            unit(2, 1024, (0, rows(sg_out[0], 2 * k, 2, 0, 1024)))
        return base

    u_ffn = [0] * 4
    u_ffn[0] = ffn_units(0, 0)
    u_ab = ab_units()
    u_ffn[1] = ffn_units(0, 1)
    u_ffn[2] = ffn_units(1, 0)
    u_sg = sg_units()
    u_ffn[3] = ffn_units(1, 1)
    N_UNITS = len(units)
    arrivals, per_slot = [], [0] * SLOTS
    for j, (_, _, pieces) in enumerate(units):
        per_slot[j % SLOTS] += len(pieces)
        arrivals.append(per_slot[j % SLOTS])

    N_ROWS = 107

    ctx = ExitStack()
    with ctx:
        def sb(name, shape, dt=f32):
            return ctx.enter_context(nc.sbuf_tensor(name, shape, dt))

        sems = {}

        def S(name):
            if name not in sems:
                sems[name] = ctx.enter_context(nc.semaphore(name))
            return sems[name]

        X = sb("X", [P, NT, D_MODEL])
        C = sb("C", [P, n_const])
        param_rows = sb("param_rows", [N_ROWS, P])
        param_cols = sb("param_cols", [P, N_ROWS])
        pos_rows = sb("pos_rows", [NT, 2, P])
        raw = sb("raw", [P, SLOTS, SLOT])
        whi = sb("whi", [P, SLOTS, SLOT], f32r)
        wlo = sb("wlo", [P, SLOTS, SLOT], f32r)
        small = sb("small", [P, 1010])
        with ExitStack() as over:
            hTh = over.enter_context(nc.sbuf_tensor("hTh", [P, KF, SEQ], f32r))
            hTl = over.enter_context(nc.sbuf_tensor("hTl", [P, KF, SEQ], f32r))
            xTh = over.enter_context(nc.sbuf_tensor("xTh", [P, KD, SEQ], f32r))
            xTl = over.enter_context(nc.sbuf_tensor("xTl", [P, KD, SEQ], f32r))
        H1 = KF * SEQ
        XT0 = 2 * H1
        R0 = XT0 + 2 * KD * SEQ
        arena = sb("arena", [P, R0 + 8544])

        def at(off, *dims):
            n = int(np.prod(dims))
            v = arena[:, off:off + n]
            if len(dims) == 2:
                v = v.rearrange("p (a b) -> p a b", b=dims[1])
            if len(dims) == 3:
                v = v.rearrange("p (a b c) -> p a b c", b=dims[1], c=dims[2])
            return v

        cursor = [0]

        def tiny(*dims):
            n = int(np.prod(dims))
            v = small[:, cursor[0]:cursor[0] + n]
            cursor[0] += n
            if len(dims) == 2:
                v = v.rearrange("p (a b) -> p a b", b=dims[1])
            if len(dims) == 3:
                v = v.rearrange("p (a b c) -> p a b c", b=dims[1], c=dims[2])
            return v

        def const(name):
            o, n = const_at[name]
            return C[:, o:o + n]

        normT = param_cols[:, 0:48].rearrange("p (s k) -> p s k", k=KD)
        convT = param_cols[:, 48:96].rearrange("p (j b) -> p b j", j=CONV)
        qn_col, kvn_col = param_cols[:, 96:98], param_cols[:, 98:99]
        bsT = param_cols[:, 99:107]
        ident, cumul, ones64 = const("ident"), const("cumul"), const("ones")

        s_buf = at(R0, NT, 512)
        h_buf = at(R0 + 1024, NT, 512)
        squares = [at(R0, 1024), at(R0 + 1024, 1024)]
        wsT = at(4096, GROUPS, P)
        V = at(R0 + 4096, NT, SGW)
        v_norm_row = at(R0 + 2048, SGW)
        ws_raw = at(0, GROUPS, P)
        xs = at(0, NT, D_MODEL)
        qTm, kTm = at(0, HEADS, SEQ), at(2048, HEADS, SEQ)
        tmp, k_sq = at(4096, 1536), at(0, NT, HEADS * NOPE)
        scores = at(H1, 3, P)
        probs = at(H1 + 384, 3, P)
        qm = at(6400, NT, HEADS * QK)
        kvm = at(7936, NT, HEADS * 128)
        pT = at(9984, 2, 3 * P)
        km = at(R0, NT, HEADS * QK)
        PM = at(R0 + 1536, NT, AW)
        Y = at(R0 + 2400, NT, D_MODEL)
        SZ = at(R0 + 4448, NT, 512)
        QKVn = [at(R0 + 5472 + 1024 * i, NT, 512) for i in range(3)]
        yc = at(2048, 2, 2, SEQ)
        (gU, Dec, DecB, Lm, Am, LT, AT) = [at(1024 * i, 1024) for i in range(7)]
        kbe, kt = at(9216, 1024), at(10240, 1024)
        LoffB, M1B = at(1024, 16, P), at(3072, 16, P)
        DB, DTB = at(7168, 16, P), at(R0 + 5472, 16, P)
        kT, qT, qdT, wT = [at(XT0 + 1024 * i, PAIRS, SEQ) for i in range(4)]
        qd = at(R0, NT, 512)
        state = at(R0 + 1024, PAIRS, P)
        v_new = at(3072, 512)
        s_dec = at(3584, PAIRS, P)

        sumsq, rstd = tiny(2), tiny(2)
        rs_a, rs_t, rs_y = tiny(32), tiny(32), tiny(32)
        c_ss, c_rs = tiny(4), tiny(4)
        head_ss = tiny(16)
        qk_ss = tiny(2, NT * HEADS)
        pe_ss = tiny(NT)
        k_pe, rope_tmp = tiny(NT, ROPE), tiny(4, NT, HALF)
        q_scale, q_nscale = tiny(NT, HEADS), tiny(NT, HEADS)
        qkn_q, qkn_k, gdn_w = tiny(QK), tiny(QK), tiny(DK)
        cosT, sinT, ang, angk = tiny(NT, HALF), tiny(NT, HALF), tiny(NT, HALF), tiny(NT, HALF)
        pos_f = tiny(NT)
        alog, dtb = tiny(HEADS), tiny(HEADS)
        beta, gdec, gc, egc, begc, ek, sp = [tiny(NT, HEADS) for _ in range(7)]
        eg = tiny(4, PAIRS)
        smax, nbias, row_sum, rden = tiny(3), tiny(2), tiny(NT, HEADS), tiny(NT, HEADS)
        v_ss = tiny(4)

        B = [ctx.enter_context(nc.psum_tensor(f"B{i}", [P, 512], f32)) for i in range(8)]

        def bc(ap, shape):
            return ap.broadcast_to(shape)

        def unit_view(ring, j, kt, width):
            return ring[:, j % SLOTS, 0:kt * width].rearrange("p (k n) -> p k n", n=width)

        X_BANK = [4, 5, 2, 3]
        N_LIVE = {"ffn0": 33, "ab": u_ffn[1]}.get(stop_after, N_UNITS)
        FFN_SUB = [0, 2, 3, 5]
        HT_FREE = 2
        D_BANK = ((6, 7), (0, 1))
        N_SMALL = 5
        B_UNIT, Z_UNIT = u_ab + 5, u_ab + 10
        C_UNIT = [u_ab + i for i in (2, 3, 4, 7, 8, 9)]
        XT = [0, 1, 3, 4, 5, 6]
        HT = {0: 0, 2: 11, 3: 22, 4: 33, 5: 41}

        block = ctx.enter_context(nc.Block())

        @block.sync
        def _(sp_):
            def load(dst, src, name):
                sp_.dma_start(dst, src).then_inc(S(name), 16)

            load(X[:], x[0].rearrange("(t p) d -> p t d", p=P), "x_loaded")
            load(C[:], const_dram, "const_loaded")

            def load_unit(j, shift=None):
                kt, width, pieces = units[j]
                turn = 0 if shift is None else shift[0]
                if j >= SLOTS:
                    sp_.wait_ge(S("lo_ready"), turn * SLOTS + (j - SLOTS + 1))
                for c0, src in (pieces if shift is None else [(0, shift[1])]):
                    dst = unit_view(raw, j, kt, width)[:, :, c0:c0 + src.shape[2]]
                    sp_.dma_start(dst, src).then_inc(S(f"raw_loaded{j % SLOTS}"), 16)

            def ffn_loads(base, l, s):
                for j in range(base, base + 4):
                    load_unit(j)
                with sp_.Fori(0, 4) as turn:
                    i = 4
                    for w in (w_gate, w_up):
                        for k0 in (0, 4):
                            src = w[l, s, k0 * P:(k0 + 4) * P, :].rearrange("(k p) n -> p k n", p=P)
                            load_unit(base + i, (turn, src[:, :, ds(turn * 512 + 512, 512)]))
                            i += 1
                for j in range(base + 20, base + 33):
                    load_unit(j)

            ffn_loads(u_ffn[0], 0, 0)
            if stop_after == "ffn0":
                pass
            else:
                for j in range(u_ab, u_ab + 16):
                    load_unit(j)
            if stop_after not in ("ffn0", "ab"):
                ffn_loads(u_ffn[1], 0, 1)
                ffn_loads(u_ffn[2], 1, 0)
                for j in range(u_sg, u_sg + 24):
                    load_unit(j)
                ffn_loads(u_ffn[3], 1, 1)
            n_x = {"ffn0": 1, "ab": 2}.get(stop_after, 6)
            for t in range(NT):
                sp_.wait_ge(S("x_updated"), 4 * (n_x - 1) + 2 * (t + 1))
                sp_.dma_start(out[0, t * P:(t + 1) * P, :], X[:, t, :]).then_inc(S("out_stored"), 16)
            sp_.wait_ge(S("out_stored"), 32)

        @block.gpsimd
        def _(pool):
            def load(dst, src, name):
                pool.dma_start(dst, src).then_inc(S(name), 16)

            if stop_after == "ffn0":
                return
            for dst, src, n in ((qkn_q, qk_norm_q, QK), (qkn_k, qk_norm_k, QK), (gdn_w, gdn_norm, DK),
                                (alog, a_log, HEADS), (dtb, dt_bias, HEADS)):
                load(dst, bc(src, [P, n]), "small_loaded")

            def after(ins):
                pool_links[0] += 1
                ins.then_inc(S("pool_chain"), 1)
                pool.wait_ge(S("pool_chain"), pool_links[0])

            pool_links = [0]
            mul = lambda o, a, b: nc.gpsimd.tensor_tensor(o, a, b, ALU.mult)
            pool.wait_ge(S("small_loaded"), 16 * N_SMALL)
            after(mul(qkn_q[:, 0:NOPE], qkn_q[:, 0:NOPE], qkn_k[:, 0:NOPE]))
            pool.wait_ge(S("pm_out"), 2)
            pool.wait_ge(S("sines_ready"), 1)
            after(mul(k_pe, PM[:, :, Q_LORA + KV_LORA:AB_W], bc(qkn_k[:, NOPE:QK].unsqueeze(1), [P, NT, ROPE])))
            r1, r2 = k_pe[:, :, 0:HALF], k_pe[:, :, HALF:ROPE]
            for i, (r, a) in enumerate(((r1, cosT), (r2, sinT), (r2, cosT), (r1, sinT))):
                after(mul(rope_tmp[:, i], r, a))
            after(nc.gpsimd.tensor_tensor(r1, rope_tmp[:, 0], rope_tmp[:, 1], ALU.subtract))
            after(nc.gpsimd.tensor_tensor(r2, rope_tmp[:, 2], rope_tmp[:, 3], ALU.add))
            pool.wait_ge(S("q_squared"), 1)
            mul(qm.rearrange("p t (h d) -> p (t h) d", d=QK), qm.rearrange("p t (h d) -> p (t h) d", d=QK),
                bc(qkn_q.unsqueeze(1), [P, NT * HEADS, QK])).then_inc(S("q_weighted"), 1)
            k4 = km.rearrange("p t (h d) -> p t h d", d=QK)
            kv4 = kvm.rearrange("p t (h d) -> p t h d", d=128)
            k_rs = qk_ss[:, 1, :].rearrange("p (t h) -> p t h", t=NT)
            pool.wait_ge(S("kv_out"), 4)
            pool.wait_ge(S("qk_rms"), 1)
            for t in range(NT):
                mul(k4[:, t, :, 0:NOPE], kv4[:, t, :, 0:NOPE], bc(k_rs[:, t, :].unsqueeze(2), [P, HEADS, NOPE])
                    ).then_inc(S("k_ready"), 1)
                mul(k4[:, t, :, NOPE:QK], bc(k_pe[:, t:t + 1, :], [P, HEADS, ROPE]),
                    bc(k_rs[:, t, :].unsqueeze(2), [P, HEADS, ROPE])).then_inc(S("k_ready"), 1)
            pool.wait_ge(S("z_out"), 2)
            z4 = SZ.rearrange("p t (h d) -> p (t h) d", d=DK)
            nc.gpsimd.tensor_tensor(z4, z4, bc(gdn_w.unsqueeze(1), [P, NT * HEADS, DK]), ALU.mult
                                    ).then_inc(S("z_weighted"), 1)
            HC = [slice(0, 64), slice(64, 128)]

            def clear(block_diagonal, name):
                for c in range(2):
                    if c:
                        pool.wait_ge(S(name), 1)
                    nc.gpsimd.memset(block_diagonal[HC[c], :, HC[1 - c]], 0.0).then_inc(S(name), 1)

            pool.wait_ge(S("z_weighted"), 1)
            pool.wait_ge(S("y_mla"), 2)
            clear(DB, "d_clear")
            pool.wait_ge(S("gdn_in"), 3)
            pool.wait_ge(S("dT_sums"), 4)
            pool.wait_ge(S("d_clear"), 2)
            clear(DTB, "dt_clear")
            pool.wait_ge(S("la_ready"), 4)
            pool.wait_ge(S("dt_clear"), 2)
            clear(LoffB, "loff_clear")
            pool.wait_ge(S("lt_ready"), 4)
            for n, b in enumerate(LEVELS[1:]):
                for t in range(NT):
                    if n:
                        pool.wait_ge(S("m1_sums"), 4 * (n - 1) + 2 * t + 2)
                    for c in range(2):
                        m = slice(8 * t, 8 * t + 8)
                        if n == 0 and t == 0 and c == 0:
                            pool.wait_ge(S("loff_clear"), 2)
                        else:
                            pool.wait_ge(S("loff_ready"), 4 * n + 2 * t + c)
                        nc.gpsimd.tensor_tensor(
                            LoffB[HC[c], m, HC[c]], LT.rearrange("p (m i) -> p m i", i=64)[HC[c], m, :],
                            bc(const(f"level{b}")[HC[c], :].unsqueeze(1), [64, 8, 64]), ALU.mult
                        ).then_inc(S("loff_ready"), 1)
            if stop_after == "ab":
                return
            pool.wait_ge(S("x_updated"), 8)
            load(v_norm_row, bc(sg_norm, [P, SGW]), "sg_loaded")
            pool.wait_ge(S("x_updated"), 16)
            load(ws_raw, sg_ws[0].rearrange("g i j -> i g j"), "sg_loaded")
            pool.wait_ge(S("sg_loaded"), 32)
            nc.gpsimd.tensor_tensor(ws_raw, ws_raw, bc(const("tril128").unsqueeze(1), [P, GROUPS, P]),
                                    ALU.mult).then_inc(S("ws_masked"), 1)
            for c in range(4):
                pool.wait_ge(S("v_scaled"), c + 1)
                nc.gpsimd.tensor_tensor(V[:, :, 512 * c:512 * c + 512], V[:, :, 512 * c:512 * c + 512],
                                        bc(v_norm_row[:, 512 * c:512 * c + 512].unsqueeze(1), [P, NT, 512]),
                                        ALU.mult).then_inc(S("v_ready"), 1)

        @block.scalar
        def _(act):
            A = nc.scalar.activation

            def hi(j, turn=0):
                if j >= N_LIVE:
                    return
                kt, width, _ = units[j]
                act.wait_ge(S(f"raw_loaded{j % SLOTS}"), turn * 16 + 16 * arrivals[j])
                if j >= SLOTS:
                    act.wait_ge(S("unit_done"), turn * SLOTS + (j - SLOTS + 1))
                A(whi[:, j % SLOTS, 0:kt * width], raw[:, j % SLOTS, 0:kt * width], ACT.Copy
                  ).then_inc(S("hi_ready"), 1)

            def x_hi(xi, norm=None):
                for k in range(KD):
                    act.wait_ge(S("xT_sums"), 4 * xi + k // 2 + 1)
                    A(xTh[:, k, :], B[X_BANK[k // 2]][:, 256 * (k % 2):256 * (k % 2) + 256], ACT.Copy,
                      scale=1.0 if norm is None else normT[:, norm, k:k + 1]).then_inc(S("xT_hi"), 1)

            def x_squares(s):
                for t in range(NT):
                    if s > 0:
                        act.wait_ge(S("x_updated"), 4 * (s - 1) + 2 * (t + 1))
                    A(squares[t], X[:, t, :], ACT.Square, accum_out=sumsq[:, t:t + 1]).then_inc(S("x_squared"), 1)

            def hT_hi(done, k0, n_blocks, turn=None):
                for b in range(0, n_blocks, 2):
                    act.wait_ge(S("hT_sums"), (0 if turn is None else turn * 2) + (done + b // 2 + 1))
                    dst = hTh[:, k0 + b:k0 + b + 2, :] if turn is None else hTh[:, ds(turn * 4 + b, 2), :]
                    A(dst, B[4 + b // 2][:].rearrange("p (b n) -> p b n", n=SEQ), ACT.Copy
                      ).then_inc(S("hT_hi"), 1)

            def silu_gate(f, c, width, turn=0):
                act.wait_ge(S("unit_done"), turn * SLOTS + u_ffn[f] + (4 * c + 2 if c < 5 else 21))
                if c == 0:
                    act.wait_ge(S("rstd_ready"), FFN_SUB[f] + 1)
                else:
                    act.wait_ge(S("h_ready"), turn * 2 + (12 * f + 2 * c))
                for t in range(NT):
                    A(s_buf[:, t, 0:width], B[t][:, 0:width], ACT.Silu, scale=rstd[:, t:t + 1]
                      ).then_inc(S("silu_done"), 1)

            def ffn(f):
                s, base = FFN_SUB[f], u_ffn[f]
                x_hi(XT[s], s)
                hi(base + 3)
                x_squares(s)
                hi(base + 4)
                silu_gate(f, 0, 512)
                for j in (5, 6, 7):
                    hi(base + j)
                with act.Fori(0, 4) as turn:
                    hi(base + 8, turn)
                    silu_gate(f, 1, 512, turn)
                    hi(base + 9, turn)
                    hT_hi(HT[s], 0, 4, turn)
                    hi(base + 10, turn)
                    hi(base + 11, turn)
                silu_gate(f, 5, 256)
                hi(base + 24)
                hT_hi(HT[s] + 8, 16, 4)
                hi(base + 25)
                hT_hi(HT[s] + 10, 20, 2)
                for j in range(26, 36):
                    hi(base + j)

            for r0, src in ((0, norm_w.rearrange("l s (k p) -> (l s k) p", p=P)),
                            (48, conv_w[0].rearrange("j (b p) -> (j b) p", p=P)),
                            (96, q_norm[0].rearrange("(b p) -> b p", p=P)),
                            (98, kv_norm), (99, sg_bs[0])):
                act.dma_start(param_rows[r0:r0 + src.shape[0], :], src).then_inc(S("rows_loaded"), 16)
            act.dma_start(pos_rows[:, 0, :].bitcast(i32), positions[0].rearrange("(t p) -> t p", p=P)
                          ).then_inc(S("pos_loaded"), 16)
            for j in range(3):
                hi(j)
            act.wait_ge(S("param_sums"), 1)
            A(param_cols[:], B[7][:, 0:N_ROWS], ACT.Copy).then_inc(S("params_ready"), 1)
            act.wait_ge(S("angles"), 1)
            A(sinT, ang, ACT.Sin).then_inc(S("sines"), 1)
            A(cosT, ang, ACT.Sin, scale=0.5).then_inc(S("sines"), 1)
            act.wait_ge(S("params_ready"), 1)
            act.wait_ge(S("x_loaded"), 16)
            ffn(0)
            if stop_after == "ffn0":
                return

            b = u_ab
            x_squares(1)
            act.wait_ge(S("small_loaded"), 16 * N_SMALL)
            x_hi(XT[1], 1)
            hi(b + 3)
            act.wait_ge(S("unit_done"), b + 2)
            for t in range(NT):
                A(PM[:, t, :], B[t][:, 0:AW], ACT.Copy).then_inc(S("pm_out"), 1)
            LAT = Q_LORA + KV_LORA
            for t in range(NT):
                for c0, c1, dst in ((0, Q_LORA, c_ss[:, t:t + 1]), (Q_LORA, LAT, c_ss[:, 2 + t:3 + t]),
                                    (LAT, AB_W, pe_ss[:, t:t + 1])):
                    A(tmp[:, 512 * t + c0:512 * t + c1], B[t][:, c0:c1], ACT.Square, accum_out=dst
                      ).then_inc(S("c_squared"), 1)
            hi(b + 4)
            hi(b + 5)

            def tap(i):
                act.wait_ge(S("unit_done"), C_UNIT[i] + 1)
                if i >= 2:
                    act.wait_ge(S("nt_sums"), i - 1)
                for s in range(2):
                    A(yc[:, i % 2, s, :], B[2 + i % 2][:, 256 * s:256 * s + 256], ACT.Copy,
                      scale=convT[:, 2 * i + s, CONV - 1:CONV]).then_inc(S("tap_done"), 1)

            def conv_silu(i):
                act.wait_ge(S("conv_done"), 2 * i + 2)
                A(yc[:, i % 2, :, :], yc[:, i % 2, :, :], ACT.Silu).then_inc(S("yc_ready"), 1)

            def nt_out(i):
                act.wait_ge(S("nt_sums"), i + 1)
                A(QKVn[i // 2][:, :, 256 * (i % 2):256 * (i % 2) + 256],
                  B[5][:].rearrange("p (t c) -> p t c", t=NT), ACT.Copy).then_inc(S("nt_out"), 1)

            tap(0)
            hi(b + 6)
            tap(1)
            conv_silu(0)
            for k in range(3):
                act.wait_ge(S("cT_sums"), 2 if k == 2 else 1)
                A(hTh[:, k, :], (B[4][:, 256 * k:256 * k + 256] if k < 2 else B[5][:, 0:256]), ACT.Copy,
                  scale=(qn_col[:, k:k + 1] if k < 2 else kvn_col)).then_inc(S("cT_hi"), 1)
            hi(b + 7)
            conv_silu(1)
            tap(2)
            nt_out(0)
            hi(b + 8)
            act.wait_ge(S("unit_done"), B_UNIT + 1)
            for t in range(NT):
                q0, q1 = (B[6], B[7]) if t == 0 else (B[0], B[1])
                A(qm[:, t, 0:512], q0[:], ACT.Copy).then_inc(S("q_out"), 1)
                A(qm[:, t, 512:768], q1[:, 0:256], ACT.Copy).then_inc(S("q_out"), 1)
            for t in range(NT):
                act.wait_ge(*((S("kv_sums"), 1) if t == 0 else (S("unit_done"), B_UNIT + 2)))
                q0, q1 = (B[4], B[5]) if t == 0 else (B[6], B[7])
                A(kvm[:, t, 0:512], q0[:], ACT.Copy).then_inc(S("kv_out"), 1)
                A(kvm[:, t, 512:1024], q1[:], ACT.Copy).then_inc(S("kv_out"), 1)
            nt_out(1)
            conv_silu(2)
            hi(b + 9)
            act.wait_ge(S("q_out"), 4)
            A(tmp, qm.rearrange("p t n -> p (t n)"), ACT.Square).then_inc(S("q_squared"), 1)
            act.wait_ge(S("kv_out"), 4)
            A(k_sq.rearrange("p t (h d) -> p (t h) d", d=NOPE),
              kvm.rearrange("p t (h d) -> p (t h) d", d=128)[:, :, 0:NOPE], ACT.Square).then_inc(S("k_squared"), 1)
            tap(3)
            hi(b + 10)
            nt_out(2)
            conv_silu(3)
            hi(b + 11)
            tap(4)
            hi(b + 12)
            nt_out(3)
            conv_silu(4)
            tap(5)
            hi(b + 13)
            conv_silu(5)
            nt_out(4)
            act.wait_ge(S("unit_done"), Z_UNIT + 2)
            for t in range(NT):
                A(SZ[:, t, :], B[t][:], ACT.Silu).then_inc(S("z_out"), 1)
            hi(b + 14)
            hi(b + 15)
            nt_out(5)
            act.wait_ge(S("a_abs"), 1)
            A(beta, PM[:, :, AB_W:AB_W + HEADS], ACT.Exp, scale=-1.0).then_inc(S("gate_exps"), 1)
            A(gc, egc, ACT.Exp, scale=-1.0).then_inc(S("gate_exps"), 1)
            A(alog, alog, ACT.Exp).then_inc(S("gate_exps"), 1)
            act.wait_ge(S("gate_exps"), 3)
            A(gc, gc, ACT.Ln, bias=1.0).then_inc(S("gate_ln"), 1)

            def qkT_out(i):
                act.wait_ge(S("qkT_sums"), i + 1)
                dst, t, g = (qTm, kTm)[i // 4], i // 2 % 2, i % 2
                A(dst[0:QK, 4 * g:4 * g + 4, P * t:P * t + P],
                  B[(4, 6)[i % 2]][0:QK, :].rearrange("p (h n) -> p h n", n=P), ACT.Copy
                  ).then_inc(S("qkT_out"), 1)

            for i in range(8):
                qkT_out(i)
            for h in range(HEADS):
                act.wait_ge(S("softmax_in"), h + 1)
                if h:
                    act.wait_ge(S("pT_sums"), h)
                A(probs[:, 0, :], scores[:, 0, :], ACT.Exp, scale=q_scale[:, 0, h:h + 1], bias=nbias[:, 0:1],
                  accum_out=row_sum[:, 0, h:h + 1]).then_inc(S("exp_done"), 1)
                A(probs[:, 1:3, :], scores[:, 1:3, :], ACT.Exp, scale=q_scale[:, 1, h:h + 1], bias=nbias[:, 1:2],
                  accum_out=row_sum[:, 1, h:h + 1]).then_inc(S("exp_done"), 1)
                if h >= 2:
                    act.wait_ge(S("pv_sums"), h - 1)
                act.wait_ge(S("pT_sums"), h + 1)
                A(pT[:, h % 2, :], B[4][:, 0:3 * P], ACT.Copy).then_inc(S("pT_out"), 1)

            act.wait_ge(S("gc_ready"), 1)
            for c in range(2):
                for odd in range(2):
                    r = slice(64 * odd, 64 * odd + 64)
                    src = B[2 + c][r, 32:48].rearrange("p (t q o) -> p t q o", t=NT, o=2)[:, :, :, odd]
                    dst = eg[r].rearrange("p (t c) q -> p t c q", c=2)[:, :, c, :]
                    A(dst, src, ACT.Exp).then_inc(S("eg_ready"), 1)
            A(egc, gc, ACT.Exp).then_inc(S("decay_exps"), 1)
            A(ek, ek, ACT.Exp).then_inc(S("decay_exps"), 1)
            act.wait_ge(S("dec_diff"), 1)
            A(Dec, Dec, ACT.Exp, scale=-1.0).then_inc(S("dec_exp"), 1)

            for i in range(6):
                act.wait_ge(S("dT_sums"), i + 1)
                A((qT, kT, qdT)[i // 2][:, 2 * (i % 2):2 * (i % 2) + 2, :],
                  B[i % 2][:].rearrange("p (q n) -> p q n", n=SEQ), ACT.Copy).then_inc(S("dT_out"), 1)
            for n, dst in enumerate((LT, AT)):
                for t in range(NT):
                    for c in range(2):
                        r = slice(64 * c, 64 * c + 64)
                        act.wait_ge(S("la_sums"), 4 * n + 2 * t + c + 1)
                        A(dst[r, 512 * t:512 * t + 512], B[4 * n + 2 * t + c][r, :], ACT.Copy
                          ).then_inc(S("lt_ready") if n == 0 else S("at_ready"), 1)
            for n in range(5):
                for g in range(4):
                    act.wait_ge(S("m1_sums"), 4 * n + g + 1)
                    if n:
                        act.wait_ge(S("yt_sums"), 4 * (n - 1) + g + 1)
                    A(M1B[:, 4 * g:4 * g + 4, :], B[(12 * n + g) % 8][:].rearrange("p (h i) -> p h i", i=P),
                      ACT.Copy).then_inc(S("m1_ready"), 1)
            for t in range(NT):
                act.wait_ge(S("w_sums"), t + 1)
                A(wT[:, :, P * t:P * t + P], B[4 + t][:].rearrange("p (q n) -> p q n", n=P), ACT.Copy, scale=-1.0
                  ).then_inc(S("w_ready"), 1)
            for n in range(4):
                t, c = n // 2, n % 2
                r = slice(64 * c, 64 * c + 64)
                act.wait_ge(S("v_sums"), n + 1)
                A(v_new[r, :], B[0][r, :], ACT.Copy).then_inc(S("v_new_ready"), 1)
                act.wait_ge(S("o_sums"), n + 1)
                A(Y[r, t, 512:1024], B[1][r, :], ACT.Copy).then_inc(S("o_out"), 1)
            x_hi(2)
            for j in range(16, 19):
                hi(b + j)
            if stop_after == "ab":
                return

            ffn(1)
            ffn(2)

            b = u_sg
            x_hi(XT[4], 4)
            hi(b + 3)
            x_squares(4)

            def gate_out(c):
                for t in range(NT):
                    act.wait_ge(S("gate_sums"), 2 * c + t + 1)
                    for g in (2 * c, 2 * c + 1):
                        A(V[:, t, CG * g:CG * g + CG], B[6 + t][:, CG * (g % 2):CG * (g % 2) + CG],
                          ACT.Identity, bias=bsT[:, g:g + 1]).then_inc(S("gate_ready"), 1)

            for c in range(4):
                act.wait_ge(S("unit_done"), b + 2 * c + 2)
                if c == 0:
                    act.wait_ge(S("rstd_ready"), 5)
                for t in range(NT):
                    A(V[:, t, 512 * c:512 * c + 512], B[2 * (c % 2) + t][:], ACT.Gelu, scale=rstd[:, t:t + 1]
                      ).then_inc(S("v_gelu"), 1)
                if c:
                    act.wait_ge(S("v_scaled"), c)
                act.wait_ge(S("v_gelu"), 2 * c + 2)
                for t in range(NT):
                    for g in range(2):
                        A(squares[t][:, CG * g:CG * g + CG], V[:, t, 512 * c + CG * g:512 * c + CG * g + CG],
                          ACT.Square, accum_out=v_ss[:, 2 * t + g:2 * t + g + 1]).then_inc(S("v_squared"), 1)
                hi(b + 2 * c + 4)
                hi(b + 2 * c + 5)
                if c == 0:
                    for n in range(2):
                        act.wait_ge(S("wsT_sums"), n + 1)
                        A(wsT[:, 4 * n:4 * n + 4, :], B[6 + n][:].rearrange("p (g n) -> p g n", n=P), ACT.Copy
                          ).then_inc(S("wsT_ready"), 1)
                else:
                    gate_out(c - 1)
            for c in range(4):
                act.wait_ge(S("unit_done"), b + 8 + 2 * c + 2)
                if c == 0:
                    act.wait_ge(S("v_scaled"), 4)
                else:
                    act.wait_ge(S("y_ready"), c)
                for t in range(NT):
                    A(s_buf[:, t, :], B[2 * (c % 2) + t][:], ACT.Gelu, scale=rstd[:, t:t + 1]
                      ).then_inc(S("u_gelu"), 1)
                if c == 0:
                    gate_out(3)
                hi(b + 8 + 2 * c + 4)
                hi(b + 8 + 2 * c + 5)
                if c >= 1:
                    hT_hi(HT[4] + 2 * (c - 1), 4 * (c - 1), 4)
            hT_hi(HT[4] + 6, 12, 4)
            for j in range(20, 27):
                hi(b + j)
            ffn(3)

        @block.vector
        def _(dve):
            TT, TS, STT = nc.vector.tensor_tensor, nc.vector.tensor_scalar, nc.vector.scalar_tensor_tensor
            links = [0]

            def link(ins):
                links[0] += 1
                ins.then_inc(S("dve_chain"), 1)
                dve.wait_ge(S("dve_chain"), links[0])

            def rsqrt(dst, ss, n, inv):
                a, u, y = rs_a[:, 0:n], rs_t[:, 0:n], rs_y[:, 0:n]
                link(TS(u, ss, inv, EPS, ALU.mult, ALU.add))
                TS(a, ss, -0.5 * inv, -0.5 * EPS, ALU.mult, ALU.add).then_inc(S("minus_half"), 1)
                halves[0] += 1
                link(TS(u.bitcast(i32), u.bitcast(i32), 1, None, ALU.logical_shift_right))
                link(TS(y.bitcast(i32), u.bitcast(i32), -1.0, float(0x5F3759DF), ALU.mult, ALU.add))
                dve.wait_ge(S("minus_half"), halves[0])
                for step in range(3):
                    link(TT(u, y, y, ALU.mult))
                    link(TT(u, u, a, ALU.mult))
                    ins = STT(dst if step == 2 else y, u, 1.5, y, ALU.add, ALU.mult)
                    if step < 2:
                        link(ins)
                return ins

            halves = [0]

            def lo(j, turn=0):
                if j >= N_LIVE:
                    return
                kt, width, _ = units[j]
                dve.wait_ge(S("hi_ready"), turn * SLOTS + (j + 1))
                n = kt * width
                TT(wlo[:, j % SLOTS, 0:n], raw[:, j % SLOTS, 0:n], whi[:, j % SLOTS, 0:n].bitcast(f32),
                   ALU.subtract).then_inc(S("lo_ready"), 1)

            def x_lo(xi, norm=None):
                for k in range(KD):
                    dve.wait_ge(S("xT_hi"), 8 * xi + 2 * (k // 2) + 2)
                    STT(xTl[:, k, :], B[X_BANK[k // 2]][:, 256 * (k % 2):256 * (k % 2) + 256],
                        1.0 if norm is None else normT[:, norm, k:k + 1], xTh[:, k, :].bitcast(f32),
                        ALU.mult, ALU.subtract).then_inc(S("xT_lo"), 1)

            def row_norm(s):
                dve.wait_ge(S("x_squared"), 2 * s + 2)
                rsqrt(rstd, sumsq, 2, 1.0 / D_MODEL).then_inc(S("rstd_ready"), 1)

            def hT_lo(done, k0, n_blocks, turn=None):
                for b in range(0, n_blocks, 2):
                    dve.wait_ge(S("hT_hi"), (0 if turn is None else turn * 2) + (done + b // 2 + 1))
                    if turn is None:
                        dst, top = hTl[:, k0 + b:k0 + b + 2, :], hTh[:, k0 + b:k0 + b + 2, :]
                    else:
                        dst, top = hTl[:, ds(turn * 4 + b, 2), :], hTh[:, ds(turn * 4 + b, 2), :]
                    TT(dst, B[4 + b // 2][:].rearrange("p (b n) -> p b n", n=SEQ), top.bitcast(f32),
                       ALU.subtract).then_inc(S("hT_lo"), 1)

            def up_product(f, c, width, turn=0):
                dve.wait_ge(S("unit_done"), turn * SLOTS + u_ffn[f] + (4 * c + 4 if c < 5 else 22))
                for t in range(NT):
                    dve.wait_ge(S("silu_done"), turn * 2 + (12 * f + 2 * c + t + 1))
                    STT(h_buf[:, t, 0:width], B[2 + t][:, 0:width], rstd[:, t:t + 1], s_buf[:, t, 0:width],
                        ALU.mult, ALU.mult).then_inc(S("h_ready"), 1)

            def x_update(s, end_unit, factor):
                dve.wait_ge(S("tok0_done"), s + 1)
                for t in range(NT):
                    if t:
                        dve.wait_ge(S("unit_done"), end_unit)
                    for n in range(2):
                        xv = X[:, t, 512 * n:512 * n + 512]
                        STT(xv, B[D_BANK[t][n]][:], factor, xv, ALU.mult, ALU.add).then_inc(S("x_updated"), 1)

            def ffn(f):
                s, base = FFN_SUB[f], u_ffn[f]
                x_lo(XT[s], s)
                lo(base + 3)
                row_norm(s)
                for j in (4, 5, 6):
                    lo(base + j)
                up_product(f, 0, 512)
                lo(base + 7)
                with dve.Fori(0, 4) as turn:
                    lo(base + 8, turn)
                    lo(base + 9, turn)
                    hT_lo(HT[s], 0, 4, turn)
                    lo(base + 10, turn)
                    up_product(f, 1, 512, turn)
                    lo(base + 11, turn)
                lo(base + 24)
                hT_lo(HT[s] + 8, 16, 4)
                up_product(f, 5, 256)
                lo(base + 25)
                hT_lo(HT[s] + 10, 20, 2)
                for j in range(26, 36):
                    lo(base + j)
                x_update(s, base + 33, 0.5)

            nc.vector.memset(rs_a, 0.0).then_inc(S("hT_lo"), HT_FREE)
            for j in range(3):
                lo(j)
            dve.wait_ge(S("pos_loaded"), 16)
            nc.vector.tensor_copy(pos_rows[:, 1, :], pos_rows[:, 0, :].bitcast(i32)).then_inc(S("pos_float"), 1)
            dve.wait_ge(S("pos_sums"), 1)
            link(nc.vector.tensor_copy(pos_f, B[6][:, 0:NT]))
            fr = const("freq")
            link(TT(ang, bc(pos_f.unsqueeze(2), [P, NT, HALF]), bc(fr.unsqueeze(1), [P, NT, HALF]), ALU.mult))
            two_pi = 2 * np.pi
            p1 = float(np.float32(6.28125))
            p2 = float(np.float32(np.round((two_pi - p1) * 2 ** 21) / 2 ** 21))
            p3 = float(np.float32(two_pi - p1 - p2))
            link(TS(angk, ang, 1.0 / two_pi, 12582912.0, ALU.mult, ALU.add))
            link(TS(angk, angk, -12582912.0, None, ALU.add))
            for part in (p1, p2, p3):
                link(STT(ang, angk, -part, ang, ALU.mult, ALU.add))
            edge = float(np.nextafter(np.float32(np.pi), np.float32(0)))
            TS(ang, ang, edge, -edge, ALU.min, ALU.max).then_inc(S("angles"), 1)
            dve.wait_ge(S("sines"), 2)
            link(TT(cosT, cosT, cosT, ALU.mult))
            TS(cosT, cosT, -2.0, 1.0, ALU.mult, ALU.add).then_inc(S("sines_ready"), 1)
            dve.wait_ge(S("params_ready"), 1)
            ffn(0)
            if stop_after == "ffn0":
                return

            b = u_ab
            dve.wait_ge(S("small_loaded"), 16 * N_SMALL)
            row_norm(1)
            dve.wait_ge(S("rstd_ready"), 2)
            for t in range(NT):
                TS(xs[:, t, :], X[:, t, :], rstd[:, t:t + 1], None, ALU.mult).then_inc(S("xs_ready"), 1)
            x_lo(XT[1], 1)
            lo(b + 3)
            lo(b + 4)
            LAT = Q_LORA + KV_LORA
            dve.wait_ge(S("c_squared"), 6)
            link(TS(c_ss[:, 2:4], c_ss[:, 2:4], float(Q_LORA // KV_LORA), None, ALU.mult))
            link(rsqrt(c_rs, c_ss, 4, 1.0 / Q_LORA))
            for t in range(NT):
                for i, (c0, c1) in enumerate(((0, Q_LORA), (Q_LORA, LAT))):
                    TS(PM[:, t, c0:c1], PM[:, t, c0:c1], c_rs[:, 2 * i + t:2 * i + t + 1], None, ALU.mult
                       ).then_inc(S("c_normed"), 1)
            lo(b + 5)

            def conv(i):
                for s in range(2):
                    dve.wait_ge(S("tap_done"), 2 * i + 2)
                    src = B[2 + i % 2][:, 256 * s:256 * s + 256]
                    for back in (1, 2, 3):
                        y = yc[:, i % 2, s, back:SEQ]
                        w = convT[:, 2 * i + s, CONV - 1 - back:CONV - back]
                        ins = STT(y, src[:, 0:SEQ - back], w, y, ALU.mult, ALU.add)
                        if back < 3:
                            link(ins)
                    ins.then_inc(S("conv_done"), 1)

            conv(0)
            lo(b + 6)
            for k in range(3):
                dve.wait_ge(S("cT_hi"), (2, 2, 3)[k])
                STT(hTl[:, k, :], (B[4][:, 256 * k:256 * k + 256] if k < 2 else B[5][:, 0:256]),
                    (qn_col[:, k:k + 1] if k < 2 else kvn_col), hTh[:, k, :].bitcast(f32),
                    ALU.mult, ALU.subtract).then_inc(S("cT_lo"), 1)
            conv(1)
            lo(b + 7)
            conv(2)
            lo(b + 8)
            lo(b + 9)
            M = NT * HEADS
            dve.wait_ge(S("q_squared"), 1)
            link(nc.vector.tensor_reduce(qk_ss[:, 0, :], tmp.rearrange("p (m d) -> p m d", d=QK), AX.X, ALU.add))
            conv(3)
            lo(b + 10)
            dve.wait_ge(S("k_squared"), 1)
            link(nc.vector.tensor_reduce(qk_ss[:, 1, :], k_sq.rearrange("p t (h d) -> p (t h) d", d=NOPE),
                                         AX.X, ALU.add))
            k_ss = qk_ss[:, 1, :].rearrange("p (t h) -> p t h", t=NT)
            link(TT(k_ss, k_ss, bc(pe_ss.unsqueeze(2), [P, NT, HEADS]), ALU.add))
            qk_rs = qk_ss.rearrange("p a m -> p (a m)")
            rsqrt(qk_rs, qk_rs, 2 * M, 1.0 / QK).then_inc(S("qk_rms"), 1)
            lo(b + 11)
            conv(4)
            lo(b + 12)
            for dst, sign in ((q_scale, 1.0), (q_nscale, -1.0)):
                TS(dst.rearrange("p t h -> p (t h)"), qk_ss[:, 0, :], sign * float(QK) ** -0.5, None, ALU.mult
                   ).then_inc(S("q_scaled"), 1)
            dve.wait_ge(S("q_weighted"), 1)
            v = [tmp[:, 256 * i:256 * i + 256].rearrange("p (t h d) -> p t h d", t=NT, h=HEADS) for i in range(4)]
            m4 = qm.rearrange("p t (h d) -> p t h d", d=QK)
            r1, r2 = m4[:, :, :, NOPE:NOPE + HALF], m4[:, :, :, NOPE + HALF:QK]
            cb, sb_ = (bc(a.unsqueeze(2), [P, NT, HEADS, HALF]) for a in (cosT, sinT))
            for i, (r, a) in enumerate(((r1, cb), (r2, sb_), (r2, cb), (r1, sb_))):
                link(TT(v[i], r, a, ALU.mult))
            link(TT(r1, v[0], v[1], ALU.subtract))
            TT(r2, v[2], v[3], ALU.add).then_inc(S("q_ready"), 1)
            conv(5)
            lo(b + 13)
            lo(b + 14)
            lo(b + 15)
            link(TT(sp, PM[:, :, AB_W + HEADS:AW], bc(dtb.unsqueeze(1), [P, NT, HEADS]), ALU.add))
            STT(egc, sp, -1.0, sp, ALU.mult, ALU.max).then_inc(S("a_abs"), 1)
            dve.wait_ge(S("gate_ln"), 1)
            link(STT(sp, sp, 0.0, gc, ALU.max, ALU.add))
            STT(gdec, sp, -1.0, bc(alog.unsqueeze(1), [P, NT, HEADS]), ALU.mult, ALU.mult
                ).then_inc(S("g_ready"), 1)
            link(TS(beta, beta, 1.0, None, ALU.add))
            link(nc.vector.reciprocal(beta, beta))

            def head_norm(a, scale):
                a3 = a.rearrange("p t (h d) -> p (t h) d", d=DK)
                t3 = yc.rearrange("p a b n -> p (a b n)").rearrange("p (m d) -> p m d", d=DK)
                link(TT(t3, a3, a3, ALU.mult))
                link(nc.vector.tensor_reduce(head_ss, t3, AX.X, ALU.add))
                link(rsqrt(head_ss, head_ss, M, 1.0))
                return STT(a3, a3, scale, bc(head_ss.unsqueeze(2), [P, M, DK]), ALU.mult, ALU.mult)

            def per_head(out_, a, w):
                return TT(out_.rearrange("p t (h d) -> p (t h) d", d=DK), a.rearrange("p t (h d) -> p (t h) d", d=DK),
                          bc(w.rearrange("p t h -> p (t h)").unsqueeze(2), [P, M, DK]), ALU.mult)

            future = const("future")
            dve.wait_ge(S("q_scaled"), 2)
            for h in range(HEADS):
                src = B[6 + h % 2][:, 0:384].rearrange("p (b n) -> p b n", n=P)
                dve.wait_ge(S("score_sums"), h + 1)
                if h:
                    dve.wait_ge(S("exp_done"), 2 * h)
                TT(scores[:, 0:2, :], src[:, 0:2, :], bc(future.unsqueeze(1), [P, 2, P]), ALU.add
                   ).then_inc(S("score_out"), 1)
                nc.vector.tensor_copy(scores[:, 2, :], src[:, 2, :]).then_inc(S("score_out"), 1)
                dve.wait_ge(S("score_out"), 2 * h + 2)
                link(nc.vector.tensor_reduce(smax, scores, AX.X, ALU.max))
                link(TT(smax[:, 1:2], smax[:, 1:2], smax[:, 2:3], ALU.max))
                TT(nbias, smax[:, 0:2], q_nscale[:, :, h], ALU.mult).then_inc(S("softmax_in"), 1)
            dve.wait_ge(S("nt_out"), 6)
            link(head_norm(QKVn[0], float(DK) ** -0.5))
            link(head_norm(QKVn[1], 1.0))
            link(per_head(QKVn[2], QKVn[2], beta))
            dve.wait_ge(S("exp_done"), 2 * HEADS)
            link(nc.vector.reciprocal(rden, row_sum))
            dve.wait_ge(S("pv_sums"), HEADS)
            for t in range(NT):
                TT(Y[:, t, 0:512].rearrange("p (h d) -> p h d", d=VDIM),
                   B[t][:].rearrange("p (h d) -> p h d", d=VDIM),
                   bc(rden[:, t, :].unsqueeze(2), [P, HEADS, VDIM]), ALU.mult).then_inc(S("y_mla"), 1)

            gf = gdec.rearrange("p t h -> p (t h)")
            TT(gU.rearrange("p (m j) -> p m j", j=64), bc(gf.unsqueeze(2), [P, M, 64]),
               bc(cumul.unsqueeze(1), [P, M, 64]), ALU.mult).then_inc(S("gu_ready"), 1)
            dve.wait_ge(S("gc_sums"), 2)
            gcf, ekf = (a.rearrange("p t h -> p (t h)") for a in (gc, ek))
            for c in range(2):
                r = slice(64 * c, 64 * c + 64)
                link(nc.vector.tensor_copy(gcf[r, :], B[2 + c][r, 0:16]))
                link(TT(ekf[r, :], B[2 + c][r, 16:32], gcf[r, :], ALU.subtract))
            link(TS(ekf, ekf, 0.0, None, ALU.add))
            nc.vector.tensor_copy(rs_a[:, 0:16], gcf).then_inc(S("gc_ready"), 1)
            D3 = Dec.rearrange("p (m j) -> p m j", j=64)
            for t in range(NT):
                for c in range(2):
                    r = slice(64 * c, 64 * c + 64)
                    dve.wait_ge(S("gr_sums"), 2 * t + c + 1)
                    link(TT(D3[r, 8 * t:8 * t + 8, :], B[4 + 2 * t + c][r, :].rearrange("p (h j) -> p h j", j=64),
                            bc(gcf[r, 8 * t:8 * t + 8].unsqueeze(2), [64, 8, 64]), ALU.subtract))
            TS(Dec, Dec, 0.0, None, ALU.max).then_inc(S("dec_diff"), 1)
            dve.wait_ge(S("decay_exps"), 2)
            link(TT(begc, beta, egc, ALU.mult))
            per_head(qd, QKVn[0], egc).then_inc(S("gdn_in"), 1)
            per_head(kbe.rearrange("p (t n) -> p t n", t=NT), QKVn[1], begc).then_inc(S("gdn_in"), 1)
            per_head(kt.rearrange("p (t n) -> p t n", t=NT), QKVn[1], ek).then_inc(S("gdn_in"), 1)
            dve.wait_ge(S("dec_exp"), 1)
            link(TT(D3, D3, bc(const("causal").unsqueeze(1), [P, M, 64]), ALU.mult))
            link(TT(DecB.rearrange("p (m j) -> p m j", j=64), D3,
                    bc(beta.rearrange("p t h -> p (t h)").unsqueeze(2), [P, M, 64]), ALU.mult))
            for n, (dst, decay) in enumerate(((Lm, DecB), (Am, Dec))):
                for odd in range(2):
                    dve.wait_ge(S("gram_sums"), 2 * n + odd + 1)
                    view = [a.rearrange("p (q o j) -> p q o j", o=2, j=64)[:, :, odd, :] for a in (dst, decay)]
                    TT(view[0], B[4 + 2 * n + odd][:].rearrange("p (q j) -> p q j", j=64), view[1], ALU.mult
                       ).then_inc(S("la_ready"), 1)
            dve.wait_ge(S("la_ready"), 4)
            m3 = lambda a: a.rearrange("p (m j) -> p m j", j=64)
            eye = bc(const("eye64").unsqueeze(1), [P, M, 64])
            HC = [slice(0, 64), slice(64, 128)]
            for src, mask, dst, clear in ((Lm, "first", DB, "d_clear"), (LT, "level1", DTB, "dt_clear")):
                if dst is DTB:
                    dve.wait_ge(S("lt_ready"), 4)
                    dve.wait_ge(S("d_ready"), 2)
                link(TT(m3(gU), m3(src), bc(const(mask).unsqueeze(1), [P, M, 64]), ALU.mult))
                dve.wait_ge(S(clear), 2)
                for r in HC:
                    TT(dst[r, :, r], eye[r, :, :], m3(gU)[r, :, :], ALU.subtract).then_inc(S("d_ready"), 1)
            for n in range(5):
                for g in range(4):
                    m = slice(4 * g, 4 * g + 4)
                    if n < 4:
                        k = 12 * n + 4 + 2 * g
                        dve.wait_ge(S("y_sums"), 4 * n + g + 1)
                        TT(DB[:, m, :], DB[:, m, :], B[k % 8][:].rearrange("p (h i) -> p h i", i=P), ALU.subtract
                           ).then_inc(S("d_merged"), 1)
                    k = 12 * n + 5 + 2 * g if n < 4 else 12 * n + 4 + g
                    dve.wait_ge(S("yt_sums"), 4 * n + g + 1)
                    TT(DTB[:, m, :], DTB[:, m, :], B[k % 8][:].rearrange("p (h i) -> p h i", i=P), ALU.subtract
                       ).then_inc(S("dt_merged"), 1)
            link(nc.vector.memset(state, 0.0))
            nc.vector.memset(v_new, 0.0).then_inc(S("state_zero"), 1)
            for n in range(3):
                for odd in range(2):
                    r, e = slice(64 * odd, 64 * odd + 64), slice(64 * odd, 64 * odd + 64)
                    decay = bc(eg[r, n, :].unsqueeze(2), [64, PAIRS, 64])
                    TT(s_dec[r, :, e], state[r, :, e], decay, ALU.mult).then_inc(S("state_decayed"), 1)
                dve.wait_ge(S("s_sums"), n + 1)
                dve.wait_ge(S("state_decayed"), 2 * n + 2)
                for odd in range(2):
                    r, e = slice(64 * odd, 64 * odd + 64), slice(64 * odd, 64 * odd + 64)
                    TT(state[r, :, e], s_dec[r, :, e],
                       B[2][r, :].rearrange("p (q e) -> p q e", e=P)[:, :, e], ALU.add
                       ).then_inc(S("state_ready"), 1)
                dve.wait_ge(S("state_ready"), 2 * n + 2)
            dve.wait_ge(S("o_out"), 4)
            O4 = Y[:, :, 512:1024].rearrange("p t (h d) -> p t h d", d=DK)
            d4 = Dec.rearrange("p (t h d) -> p t h d", t=NT, d=DK)
            link(TT(d4, O4, O4, ALU.mult))
            link(nc.vector.tensor_reduce(head_ss, m3(Dec), AX.X, ALU.add))
            link(rsqrt(head_ss, head_ss, M, 1.0 / DK))
            hs = head_ss.rearrange("p (t h) -> p t h", t=NT).unsqueeze(3)
            link(TT(O4, O4, bc(hs, [P, NT, HEADS, DK]), ALU.mult))
            dve.wait_ge(S("z_weighted"), 1)
            TT(Y[:, :, 512:1024], Y[:, :, 512:1024], SZ, ALU.mult).then_inc(S("y_gdn"), 1)
            x_lo(2)
            for j in range(16, 19):
                lo(b + j)
            x_update(1, b + 16, 1.0)
            if stop_after == "ab":
                return

            ffn(1)
            ffn(2)

            b = u_sg
            x_lo(XT[4], 4)
            lo(b + 3)
            row_norm(4)
            for c in range(4):
                lo(b + 2 * c + 4)
                dve.wait_ge(S("v_squared"), 4 * c + 4)
                link(rsqrt(v_ss, v_ss, 4, 1.0 / CG))
                v4 = V[:, :, 512 * c:512 * c + 512].rearrange("p t (g n) -> p t g n", n=CG)
                r4 = v_ss.rearrange("p (t g) -> p t g", g=2).unsqueeze(3)
                TT(v4, v4, bc(r4, [P, NT, 2, CG]), ALU.mult).then_inc(S("v_scaled"), 1)
                lo(b + 2 * c + 5)
            for c in range(4):
                lo(b + 8 + 2 * c + 4)
                if c >= 1:
                    hT_lo(HT[4] + 2 * (c - 1), 4 * (c - 1), 4)
                dve.wait_ge(S("u_gelu"), 2 * c + 2)
                dve.wait_ge(S("gate_ready"), 4 * c + 4)
                TT(h_buf, s_buf, V[:, :, 512 * c:512 * c + 512], ALU.mult).then_inc(S("y_ready"), 1)
                lo(b + 8 + 2 * c + 5)
            hT_lo(HT[4] + 6, 12, 4)
            for j in range(20, 27):
                lo(b + j)
            x_update(4, b + 24, 1.0)
            ffn(3)

        @block.tensor
        def _(pe):
            mm, transpose = nc.tensor.matmul, nc.tensor.transpose

            def split_mm(out_ap, lh, ll, rh, rl, first, last):
                mm(out_ap, lh, rh, start=first, stop=False)
                mm(out_ap, lh, rl, start=False, stop=False)
                return mm(out_ap, ll, rh, start=False, stop=last)

            def slot(j):
                kt, width, _ = units[j]
                return unit_view(whi, j, kt, width), unit_view(wlo, j, kt, width)

            def begin(j, turn=0):
                pe.wait_ge(S("lo_ready"), turn * SLOTS + (j + 1))

            def gemm(j, banks, k0, k_all, srcs, turn=0):
                kt, width, _ = units[j]
                wh, wl = slot(j)
                sh, sl = srcs
                begin(j, turn)
                for k in range(kt):
                    for t in range(NT):
                        tok = slice(P * t, P * t + P)
                        last = split_mm(B[banks[t]][:, 0:width], sh[:, k0 + k, tok], sl[:, k0 + k, tok],
                                        wh[:, k, :], wl[:, k, :], k0 + k == 0, k0 + k == k_all - 1)
                last.then_inc(S("unit_done"), 1)

            def down(base, n_units, srcs, done_before=0, upto=None):
                sh, sl = srcs
                for i in range(done_before, n_units if upto is None else upto):
                    j = base + i
                    wh, wl = slot(j)
                    begin(j)
                    final = i == n_units - 1
                    order = [(k, t) for t in range(NT) for k in range(2)] if final else \
                            [(k, t) for k in range(2) for t in range(NT)]
                    for k, t in order:
                        kk, tok = 2 * i + k, slice(P * t, P * t + P)
                        a, z = kk == 0, kk == 2 * n_units - 1
                        outs = [B[D_BANK[t][n]][:] for n in range(2)]
                        cols = [slice(0, 512), slice(512, 1024)]
                        for n in range(2):
                            mm(outs[n], sh[:, kk, tok], wh[:, k, cols[n]], start=a, stop=False)
                            mm(outs[n], sh[:, kk, tok], wl[:, k, cols[n]], start=False, stop=False)
                        for n in range(2):
                            last = mm(outs[n], sl[:, kk, tok], wh[:, k, cols[n]], start=False, stop=z)
                        if final and z and t == 0:
                            last.then_inc(S("tok0_done"), 1)
                    last.then_inc(S("unit_done"), 1)

            def x_transposes(xi, src, waits):
                for t in range(NT):
                    waits(t)
                    for k in range(KD):
                        last = transpose(B[X_BANK[k // 2]][:, 256 * (k % 2) + P * t:256 * (k % 2) + P * t + P],
                                         src[:, t, P * k:P * k + P], ident)
                        if t == NT - 1 and k % 2:
                            last.then_inc(S("xT_sums"), 1)

            def h_transposes(n_blocks, banks_read, turn=0):
                for bank in range(n_blocks // 2):
                    pe.wait_ge(S("hT_lo"), turn * 2 + (HT_FREE + banks_read + bank + 1))
                    for i in range(2):
                        for t in range(NT):
                            f = P * (2 * bank + i)
                            last = transpose(B[4 + bank][:, 256 * i + P * t:256 * i + P * t + P],
                                             h_buf[:, t, f:f + P], ident)
                    last.then_inc(S("hT_sums"), 1)

            XS, HS = (xTh, xTl), (hTh, hTl)

            def ffn(f):
                s, base = FFN_SUB[f], u_ffn[f]
                if s == 0:
                    def waits(t):
                        if t == 0:
                            pe.wait_ge(S("x_loaded"), 16)
                else:
                    def waits(t):
                        pe.wait_ge(S("x_updated"), 4 * (s - 1) + 2 * (t + 1))
                x_transposes(XT[s], X, waits)
                for i, banks in ((0, (0, 1)), (2, (2, 3))):
                    for u in range(2):
                        pe.wait_ge(S("xT_lo"), 8 * XT[s] + (4 * u + 4 if i == 0 else 8))
                        gemm(base + i + u, banks, 4 * u, KD, XS)
                with pe.Fori(0, 4) as turn:
                    pe.wait_ge(S("silu_done"), turn * 2 + (12 * f + 2))
                    gemm(base + 4, (0, 1), 0, KD, XS, turn)
                    gemm(base + 5, (0, 1), 4, KD, XS, turn)
                    pe.wait_ge(S("h_ready"), turn * 2 + (12 * f + 2))
                    h_transposes(4, HT[s] - 2, turn)
                    gemm(base + 6, (2, 3), 0, KD, XS, turn)
                    gemm(base + 7, (2, 3), 4, KD, XS, turn)
                pe.wait_ge(S("silu_done"), 12 * f + 10)
                gemm(base + 20, (0, 1), 0, KD, XS)
                pe.wait_ge(S("h_ready"), 12 * f + 10)
                h_transposes(4, HT[s] + 6)
                gemm(base + 21, (2, 3), 0, KD, XS)
                pe.wait_ge(S("silu_done"), 12 * f + 12)
                pe.wait_ge(S("hT_lo"), HT_FREE + HT[s] + 10)
                down(base + 22, 11, HS, upto=2)
                pe.wait_ge(S("h_ready"), 12 * f + 12)
                h_transposes(2, HT[s] + 8)
                down(base + 22, 11, HS, done_before=2, upto=10)
                pe.wait_ge(S("hT_lo"), HT_FREE + HT[s] + 11)
                down(base + 22, 11, HS, done_before=10)


            pe.wait_ge(S("const_loaded"), 16)
            pe.wait_ge(S("rows_loaded"), 80)
            transpose(B[7][:, 0:N_ROWS], param_rows[:], ident[0:N_ROWS, 0:N_ROWS]).then_inc(S("param_sums"), 1)
            pe.wait_ge(S("pos_float"), 1)
            transpose(B[6][:, 0:NT], pos_rows[:, 1, :], ident[0:NT, 0:NT]).then_inc(S("pos_sums"), 1)
            ffn(0)
            if stop_after == "ffn0":
                return

            b = u_ab
            x_transposes(XT[1], xs, lambda t: pe.wait_ge(S("xs_ready"), t + 1))
            for u in range(2):
                pe.wait_ge(S("xT_lo"), 8 * XT[1] + 4 * u + 4)
                gemm(b + u, (0, 1), 4 * u, KD, XS)

            def channels(i):
                j = C_UNIT[i]
                wh, wl = slot(j)
                begin(j)
                if i >= 2:
                    pe.wait_ge(S("conv_done"), 2 * (i - 1))
                for s in range(2):
                    cols = slice(P * s, P * s + P)
                    for k in range(KD):
                        last = split_mm(B[2 + i % 2][:, 256 * s:256 * s + 256], wh[:, k, cols], wl[:, k, cols],
                                        xTh[:, k, :], xTl[:, k, :], k == 0, k == KD - 1)
                last.then_inc(S("unit_done"), 1)

            def to_tokens(i):
                pe.wait_ge(S("yc_ready"), i + 1)
                if i:
                    pe.wait_ge(S("nt_out"), i)
                if i == 1:
                    pe.wait_ge(S("kv_out"), 2)
                for s in range(2):
                    for t in range(NT):
                        last = transpose(B[5][:, 256 * t + P * s:256 * t + P * s + P],
                                         yc[:, i % 2, s, P * t:P * t + P], ident)
                last.then_inc(S("nt_sums"), 1)

            channels(0)
            channels(1)
            pe.wait_ge(S("c_normed"), 4)
            for k in range(3):
                for t in range(NT):
                    dst = B[4][:, 256 * k + P * t:256 * k + P * t + P] if k < 2 else B[5][:, P * t:P * t + P]
                    last = transpose(dst, PM[:, t, P * k:P * k + P], ident)
                if k:
                    last.then_inc(S("cT_sums"), 1)
            channels(2)
            pe.wait_ge(S("cT_lo"), 3)
            to_tokens(0)
            begin(B_UNIT)
            wh, wl = slot(B_UNIT)
            for t in range(NT):
                if t:
                    pe.wait_ge(S("c_squared"), 6)
                for n, (c0, c1) in enumerate(((0, 512), (512, 768))):
                    for k in range(2):
                        tok = slice(P * t, P * t + P)
                        last = split_mm(B[(6, 0)[t] + n][:, 0:c1 - c0], hTh[:, k, tok], hTl[:, k, tok],
                                        wh[:, k, c0:c1], wl[:, k, c0:c1], k == 0, k == 1)
            last.then_inc(S("unit_done"), 1)
            begin(B_UNIT + 1)
            wh, wl = slot(B_UNIT + 1)
            for t in range(NT):
                pe.wait_ge(*((S("q_out"), 2) if t else (S("nt_out"), 1)))
                for n in range(2):
                    tok, c0 = slice(P * t, P * t + P), 512 * n
                    last = split_mm(B[(4, 6)[t] + n][:], hTh[:, 2, tok], hTl[:, 2, tok],
                                    wh[:, 0, c0:c0 + 512], wl[:, 0, c0:c0 + 512], True, True)
                if t == 0:
                    last.then_inc(S("kv_sums"), 1)
            last.then_inc(S("unit_done"), 1)
            to_tokens(1)
            channels(3)
            to_tokens(2)
            channels(4)
            to_tokens(3)
            channels(5)
            pe.wait_ge(S("q_out"), 4)
            gemm(Z_UNIT, (0, 1), 0, KD, XS)
            to_tokens(4)
            gemm(Z_UNIT + 1, (0, 1), 4, KD, XS)
            to_tokens(5)

            for i in range(8):
                src, t, g = (qm, km)[i // 4], i // 2 % 2, i % 2
                pe.wait_ge(*((S("q_ready"), 1) if i < 4 else (S("k_ready"), 4)))
                if i == 0:
                    pe.wait_ge(S("kv_out"), 4)
                if i >= 2:
                    pe.wait_ge(S("qkT_out"), i - 1)
                for h in range(4):
                    last = transpose(B[(4, 6)[i % 2]][0:QK, P * h:P * h + P],
                                     src[:, t, QK * (4 * g + h):QK * (4 * g + h) + QK], ident)
                last.then_inc(S("qkT_sums"), 1)

            def head_scores(h):
                if h < 2:
                    pe.wait_ge(S("qkT_out"), 8)
                else:
                    pe.wait_ge(S("score_out"), 2 * (h - 1))
                for i, (tq, tk) in enumerate(((0, 0), (1, 1), (1, 0))):
                    last = mm(B[6 + h % 2][:, P * i:P * i + P], qTm[0:QK, h, P * tq:P * tq + P],
                              kTm[0:QK, h, P * tk:P * tk + P], start=True, stop=True)
                last.then_inc(S("score_sums"), 1)

            head_scores(0)
            head_scores(1)
            kv_v = kvm.rearrange("p t (h d) -> p t h d", d=NOPE + VDIM)[:, :, :, NOPE:]
            for h in range(HEADS):
                pe.wait_ge(S("exp_done"), 2 * h + 2)
                if h:
                    pe.wait_ge(S("pT_out"), h)
                for i in range(3):
                    last = transpose(B[4][:, P * i:P * i + P], probs[:, i, :], ident)
                last.then_inc(S("pT_sums"), 1)
                if h + 2 < HEADS:
                    head_scores(h + 2)
                pe.wait_ge(S("pT_out"), h + 1)
                if h == 0:
                    pe.wait_ge(S("z_out"), 2)
                e = slice(VDIM * h, VDIM * h + VDIM)
                for t, i, tk, a, z in ((0, 0, 0, True, True), (1, 1, 1, True, False), (1, 2, 0, False, True)):
                    last = mm(B[t][:, e], pT[:, h % 2, P * i:P * i + P], kv_v[:, tk, h, :], start=a, stop=z)
                last.then_inc(S("pv_sums"), 1)

            HC = [slice(0, 64), slice(64, 128)]
            pe.wait_ge(S("g_ready"), 1)
            for c in range(2):
                r = HC[c]
                g2 = gdec.rearrange("p t h -> p (t h)")
                mm(B[2 + c][r, 0:16], cumul[r, :], g2[r, :], start=True, stop=True)
                mm(B[2 + c][r, 16:32], ones64[r, :], g2[r, :], start=True, stop=True)
                for r2 in HC:
                    last = mm(B[2 + c][r2, 32:48], ones64[r, :], g2[r, :], start=True, stop=True)
                last.then_inc(S("gc_sums"), 1)
            pe.wait_ge(S("gu_ready"), 1)
            for t in range(NT):
                for c in range(2):
                    if t == 0 and c == 0:
                        pe.wait_ge(S("softmax_in"), HEADS)
                    mm(B[4 + 2 * t + c][HC[c], :], ones64[HC[c], :], gU[HC[c], 512 * t:512 * t + 512],
                       start=True, stop=True).then_inc(S("gr_sums"), 1)
            pe.wait_ge(S("y_mla"), 2)
            for i, src in enumerate((QKVn[0], QKVn[1], qd)):
                if i == 2:
                    pe.wait_ge(S("gdn_in"), 1)
                for g in range(2):
                    n = 2 * i + g
                    if n >= 2:
                        pe.wait_ge(S("dT_out"), n - 1)
                    for q in range(2):
                        for t in range(NT):
                            last = transpose(B[n % 2][:, 256 * q + P * t:256 * q + P * t + P],
                                             src[:, t, P * (2 * g + q):P * (2 * g + q) + P], ident)
                    last.then_inc(S("dT_sums"), 1)
            pe.wait_ge(S("dT_out"), 4)
            pe.wait_ge(S("dec_diff"), 1)
            for n, left in enumerate((kT, qT)):
                for odd in range(2):
                    r = HC[odd]
                    for t in range(NT):
                        for q in range(PAIRS):
                            for c in range(2):
                                tok = slice(P * t + 64 * c, P * t + 64 * c + 64)
                                col = 64 * (PAIRS * t + q)
                                last = mm(B[4 + 2 * n + odd][HC[c], col:col + 64], left[r, q, tok],
                                          kT[r, q, tok], start=True, stop=True)
                    last.then_inc(S("gram_sums"), 1)
            pe.wait_ge(S("dT_out"), 6)
            eye = const("eye64")

            def problems(t, bank, lhs, rhs, name):
                for h in range(HEADS):
                    m = slice(64 * (8 * t + h), 64 * (8 * t + h) + 64)
                    for c in range(2):
                        last = mm(B[bank + c][HC[c], 64 * h:64 * h + 64], lhs[HC[c], m],
                                  (eye[HC[c], :] if rhs is None else rhs[HC[c], m]), start=True, stop=True)
                        if h == HEADS - 1:
                            last.then_inc(S(name), 1)

            pe.wait_ge(S("la_ready"), 4)
            pe.wait_ge(S("eg_ready"), 4)
            pe.wait_ge(S("gc_ready"), 1)
            for n, src in enumerate((Lm, Am)):
                for t in range(NT):
                    problems(t, 4 * n + 2 * t, src, None, "la_sums")

            def merge(g, k, lhs, rhs, name):
                for i in range(4):
                    last = mm(B[k % 8][:, P * i:P * i + P], lhs[:, 4 * g + i, :], rhs[:, 4 * g + i, :],
                              start=True, stop=True)
                last.then_inc(S(name), 1)

            for n in range(5):
                for g in range(4):
                    pe.wait_ge(S("loff_ready"), 4 * n + 2 * (g // 2) + 2)
                    if n:
                        pe.wait_ge(S("d_merged"), 4 * (n - 1) + g + 1)
                    else:
                        pe.wait_ge(S("d_ready"), 2)
                    merge(g, 12 * n + g, LoffB, DB, "m1_sums")
                for g in range(4):
                    pe.wait_ge(S("m1_ready"), 4 * n + g + 1)
                    if n:
                        pe.wait_ge(S("dt_merged"), 4 * n if g else 4 * n - 1)
                    elif g == 0:
                        pe.wait_ge(S("d_ready"), 4)
                        pe.wait_ge(S("at_ready"), 4)
                    if n < 4:
                        merge(g, 12 * n + 4 + 2 * g, DTB, M1B, "y_sums")
                        merge(g, 12 * n + 5 + 2 * g, M1B, DTB, "yt_sums")
                    else:
                        merge(g, 12 * n + 4 + g, M1B, DTB, "yt_sums")
            for t in range(NT):
                pe.wait_ge(S("dt_merged"), 18 + 2 * t)
                for h in range(HEADS):
                    q = h // 2
                    last = mm(B[4 + t][HC[h % 2], P * q:P * q + P], kbe[:, 512 * t + 64 * h:512 * t + 64 * h + 64],
                              DTB[:, 8 * t + h, :], start=True, stop=True)
                last.then_inc(S("w_sums"), 1)
            pe.wait_ge(S("w_ready"), 2)
            pe.wait_ge(S("state_zero"), 1)
            for n in range(4):
                t, c = n // 2, n % 2
                r, tok = HC[c], slice(P * t + 64 * c, P * t + 64 * c + 64)
                if n:
                    pe.wait_ge(S("v_new_ready"), n)
                for h in range(HEADS):
                    last = mm(B[0][r, 64 * h:64 * h + 64], DTB[r, 8 * t + h, r],
                       QKVn[2][r, t, 64 * h:64 * h + 64], start=h == 0, stop=n == 0, skip_group_check=True)
                if n:
                    pe.wait_ge(S("state_ready"), 2 * n)
                    pe.wait_ge(S("o_out"), n)
                    for q in range(PAIRS):
                        last = mm(B[0][r, P * q:P * q + P], wT[:, q, tok], state[:, q, :], start=False, stop=True,
                                  skip_group_check=True)
                last.then_inc(S("v_sums"), 1)
                for q in range(PAIRS):
                    if n:
                        mm(B[1][r, P * q:P * q + P], qdT[:, q, tok], state[:, q, :], start=q == 0, stop=False,
                           skip_group_check=True)
                pe.wait_ge(S("v_new_ready"), n + 1)
                for h in range(HEADS):
                    last = mm(B[1][r, 64 * h:64 * h + 64], AT[r, 64 * (8 * t + h):64 * (8 * t + h) + 64],
                              v_new[r, 64 * h:64 * h + 64], start=(n == 0 and h == 0), stop=True,
                              skip_group_check=True)
                last.then_inc(S("o_sums"), 1)
                if n < 3:
                    for q in range(PAIRS):
                        last = mm(B[2][:, P * q:P * q + P], kt[r, 512 * t + P * q:512 * t + P * q + P],
                                  v_new[r, P * q:P * q + P], start=True, stop=True)
                    last.then_inc(S("s_sums"), 1)
            x_transposes(2, Y, lambda t: pe.wait_ge(S("y_gdn"), 1))
            pe.wait_ge(S("xT_lo"), 24)
            down(b + 12, 4, XS)
            if stop_after == "ab":
                return

            ffn(1)
            ffn(2)

            b = u_sg
            x_transposes(XT[4], X, lambda t: pe.wait_ge(S("x_updated"), 12 + 2 * (t + 1)))

            def gates(c):
                pe.wait_ge(S("v_ready"), c + 1)
                if c:
                    pe.wait_ge(S("gate_ready"), 4 * c)
                else:
                    pe.wait_ge(S("wsT_ready"), 2)
                for t in range(NT):
                    for g in (2 * c, 2 * c + 1):
                        last = mm(B[6 + t][:, CG * (g % 2):CG * (g % 2) + CG], wsT[:, g, :],
                                  V[:, t, CG * g:CG * g + CG], start=True, stop=True)
                    last.then_inc(S("gate_sums"), 1)

            for c in range(8):
                for u in range(2):
                    if c == 0:
                        pe.wait_ge(S("xT_lo"), 8 * XT[4] + 4 * u + 4)
                    if c >= 2 and u == 0:
                        pe.wait_ge(S("v_gelu"), min(2 * (c - 1), 8))
                        if c >= 6:
                            pe.wait_ge(S("u_gelu"), 2 * (c - 5))
                    gemm(b + 2 * c + u, (2 * (c % 2), 2 * (c % 2) + 1), 4 * u, KD, XS)
                if c == 0:
                    pe.wait_ge(S("ws_masked"), 1)
                    for g in range(GROUPS):
                        last = transpose(B[6 + g // 4][:, P * (g % 4):P * (g % 4) + P], ws_raw[:, g, :], ident)
                        if g % 4 == 3:
                            last.then_inc(S("wsT_sums"), 1)
                elif c <= 4:
                    gates(c - 1)
                else:
                    pe.wait_ge(S("y_ready"), c - 4)
                    h_transposes(4, HT[4] + 2 * (c - 5) - 2)
            pe.wait_ge(S("gate_ready"), 16)
            pe.wait_ge(S("u_gelu"), 8)
            pe.wait_ge(S("hT_lo"), HT_FREE + HT[4] + 6)
            down(b + 16, 8, HS, upto=2)
            pe.wait_ge(S("y_ready"), 4)
            h_transposes(4, HT[4] + 4)
            down(b + 16, 8, HS, done_before=2, upto=6)
            pe.wait_ge(S("hT_lo"), HT_FREE + HT[4] + 8)
            down(b + 16, 8, HS, done_before=6)
            ffn(3)


_INS = ["x", "positions", "norm_w", "ffn_w_gate", "ffn_w_up", "ffn_w_down", "ab_w_in", "mla_q_norm",
        "mla_w_q_b", "mla_kv_norm", "mla_w_kv_b", "mla_qk_norm_q", "mla_qk_norm_k", "gdn_conv_w",
        "gdn_a_log", "gdn_dt_bias", "gdn_out_norm", "ab_w_out", "sg_w_in", "sg_v_norm", "sg_w_s",
        "sg_b_s", "sg_w_out"]


def kernel(**inputs):
    import concourse.bacc as bacc
    from concourse.bass_utils import run_bass_kernel_spmd

    nc = bacc.Bacc("TRN2", target_bir_lowering=False, num_devices=1)
    arrays, args = {}, []
    for name, a in [(n, inputs[n]) for n in _INS] + [("constants", constants()[0])]:
        a = np.ascontiguousarray(a)
        arrays[f"in_{name}"] = a
        args.append(nc.dram_tensor(f"in_{name}", a.shape, mybir.dt.from_np(a.dtype), kind="ExternalInput").ap())
    args.append(nc.dram_tensor("out_x", (1, SEQ, D_MODEL), mybir.dt.float32, kind="ExternalOutput").ap())
    build_trunk(nc, *args)
    r = run_bass_kernel_spmd(nc, [arrays], core_ids=[0])
    return r.results[0]["out_x"]
```
